# Optimizing a Trainium2 kernel written in Bass

```python
import math
import jax
import jax.numpy as jnp
from jax import lax
import numpy as np

D_MODEL = 1024
BATCH = 1
SEQ = 256
DEPTH = 2
DEC_BATCH = 8
DEC_SEQ = 8
PAST_LEN = 2048
PAGE_SIZE = 128

N_EVEN = (DEPTH + 1) // 2
N_ODD = DEPTH // 2
RET_HEADS = 4
RET_DK = D_MODEL // 8
RET_DV = D_MODEL // 8
ML_HEADS = 4
ML_DK = D_MODEL // 8
ML_DV = D_MODEL // 8
ML_CONV = 4
HG_HEADS = 8
HG_DK = D_MODEL // 8
HG_DV = D_MODEL // 8
D_FF = 2816
N_EXPERTS = 8
TOP_K = 2
D_FF_EXPERT = 2816
RET_CHUNK = 128
ML_CHUNK = 128
HG_CHUNK = 16
ROPE_BASE = 10000.0
EPS = 1e-6
FORGET_BIAS_LO = 3.0
FORGET_BIAS_HI = 6.0

RET_W = RET_HEADS * RET_DV
ML_W = ML_HEADS * ML_DV
HG_W = HG_HEADS * HG_DV
AB_SPLITS = (RET_HEADS * RET_DK, RET_HEADS * RET_DK, RET_W, RET_W,
             ML_HEADS * ML_DK, ML_HEADS * ML_DK, ML_W, ML_W, ML_HEADS, ML_HEADS)
AB_IN = sum(AB_SPLITS)
C_SPLITS = (HG_HEADS * HG_DK, HG_HEADS * HG_DK, HG_W, HG_W)
C_IN = sum(C_SPLITS)

kernel_name = 'hybrid_retnet_mlstm_hgrn2_moe_step'

def _rmsnorm(x, g):
    xf = x.astype(jnp.float32)
    y = xf * lax.rsqrt(jnp.mean(jnp.square(xf), axis=-1, keepdims=True) + EPS)
    return (y * g.astype(jnp.float32)).astype(x.dtype)

def _head_norm(o, g, center):
    if center:
        o = o - jnp.mean(o, axis=-1, keepdims=True)
    o = o * lax.rsqrt(jnp.mean(jnp.square(o), axis=-1, keepdims=True) + EPS)
    return o.reshape(o.shape[0], o.shape[1], -1) * g.astype(jnp.float32)

def _split(a, sizes):
    return jnp.split(a, np.cumsum(sizes)[:-1].tolist(), axis=-1)

def _rope(x, positions):
    half = x.shape[-1] // 2
    inv = ROPE_BASE ** (-jnp.arange(half, dtype=jnp.float32) / half)
    ang = positions.astype(jnp.float32)[:, None] * inv[None, :]
    cos = jnp.cos(ang)[None, :, None, :]
    sin = jnp.sin(ang)[None, :, None, :]
    x1, x2 = x[..., :half], x[..., half:]
    return jnp.concatenate([x1 * cos - x2 * sin, x1 * sin + x2 * cos], axis=-1)

def _to_chunks(a, c):
    B, L = a.shape[:2]
    a = a.reshape((B, L // c, c) + a.shape[2:])
    return jnp.moveaxis(jnp.moveaxis(a, 1, 0), 3, 2)

def _from_chunks(o):
    n, B, H, c = o.shape[:4]
    o = jnp.moveaxis(jnp.moveaxis(o, 2, 3), 0, 1)
    return o.reshape((B, n * c, H) + o.shape[4:])

def _causal_conv(x, buf, w, b):
    L = x.shape[1]
    xc = jnp.concatenate([buf.astype(x.dtype), x], axis=1)
    y = b
    for j in range(ML_CONV):
        y = y + xc[:, j:j + L] * w[j]
    return y, xc[:, L:]

def _retention(q, k, v, state):
    B, L, H, _ = q.shape
    c = math.gcd(L, RET_CHUNK)
    log_gamma = jnp.log1p(-jnp.exp2(-5.0 - jnp.arange(H, dtype=jnp.float32)))
    idx = jnp.arange(c, dtype=jnp.float32)
    diff = idx[:, None] - idx[None, :]
    causal = diff >= 0
    decay = jnp.where(causal[None], jnp.exp(jnp.where(causal, diff, 0.0)[None] * log_gamma[:, None, None]), 0.0)
    q_dec = jnp.exp((idx + 1.0)[None, :] * log_gamma[:, None])[..., None]
    k_dec = jnp.exp((c - 1.0 - idx)[None, :] * log_gamma[:, None])[..., None]
    chunk_dec = jnp.exp(c * log_gamma)[:, None, None]

    def step(S, inp):
        qc, kc, vc = inp
        intra = jnp.einsum('bhts,bhsv->bhtv', jnp.einsum('bhtk,bhsk->bhts', qc, kc) * decay, vc)
        inter = jnp.einsum('bhtk,bhkv->bhtv', qc, S) * q_dec
        S_new = S * chunk_dec + jnp.einsum('bhsk,bhsv->bhkv', kc * k_dec, vc)
        return S_new, intra + inter

    S, out = lax.scan(step, state, (_to_chunks(q, c), _to_chunks(k, c), _to_chunks(v, c)))
    return _from_chunks(out), S

def _mlstm(q, k, v, i_pre, log_f, C, n, m):
    B, L, H, _ = q.shape
    c = math.gcd(L, ML_CHUNK)
    causal = jnp.tril(jnp.ones((c, c), dtype=bool))

    def step(carry, inp):
        C, n, m = carry
        qc, kc, vc, ic, fc = inp
        b = jnp.cumsum(fc, axis=-1)
        src = ic - b
        m_t = b + jnp.maximum(m[..., None], lax.cummax(src, axis=2))
        w = jnp.exp(jnp.where(causal, b[..., :, None] + src[..., None, :] - m_t[..., :, None], -jnp.inf))
        w_prev = jnp.exp(b + m[..., None] - m_t)
        s = jnp.einsum('bhtk,bhsk->bhts', qc, kc) * w
        num = jnp.einsum('bhts,bhsv->bhtv', s, vc) + w_prev[..., None] * jnp.einsum('bhtk,bhkv->bhtv', qc, C)
        den = jnp.sum(s, axis=-1) + w_prev * jnp.einsum('bhtk,bhk->bht', qc, n)
        h = num / jnp.maximum(jnp.abs(den), jnp.exp(-m_t))[..., None]
        m_new = m_t[..., -1]
        w_end = jnp.exp(b[..., -1:] + src - m_new[..., None])
        dec = jnp.exp(b[..., -1] + m - m_new)
        C_new = dec[..., None, None] * C + jnp.einsum('bhsk,bhsv->bhkv', kc * w_end[..., None], vc)
        n_new = dec[..., None] * n + jnp.einsum('bhsk,bhs->bhk', kc, w_end)
        return (C_new, n_new, m_new), h

    (C, n, m), out = lax.scan(step, (C, n, m), (_to_chunks(q, c), _to_chunks(k, c), _to_chunks(v, c),
                                                 _to_chunks(i_pre, c), _to_chunks(log_f, c)))
    return _from_chunks(out), C, n, m

def _hgrn2(q, k, log_f, v, S):
    B, L, H, _ = q.shape
    c = math.gcd(L, HG_CHUNK)
    causal = jnp.tril(jnp.ones((c, c), dtype=bool))[..., None]

    def step(S, inp):
        qc, kc, fc, vc = inp
        A = jnp.cumsum(fc, axis=2)
        inter = jnp.einsum('bhtk,bhkv->bhtv', qc * jnp.exp(A), S)
        dec = jnp.exp(jnp.where(causal, A[:, :, :, None, :] - A[:, :, None, :, :], -jnp.inf))
        s = jnp.einsum('bhtk,bhtsk->bhts', qc, dec * kc[:, :, None, :, :])
        intra = jnp.einsum('bhts,bhsv->bhtv', s, vc)
        A_end = A[:, :, -1:, :]
        S_new = jnp.exp(A_end[:, :, 0, :])[..., None] * S + jnp.einsum('bhsk,bhsv->bhkv', kc * jnp.exp(A_end - A), vc)
        return S_new, inter + intra

    S, out = lax.scan(step, S, (_to_chunks(q, c), _to_chunks(k, c), _to_chunks(log_f, c), _to_chunks(v, c)))
    return _from_chunks(out), S

def _mixer_ab(h, positions, ret_s, mc_s, mn_s, mm_s, conv_s, w_in, b_gates, conv_w, conv_b, ret_gn, ml_gn, w_out):
    f32 = jnp.float32
    B, L, _ = h.shape
    proj = jnp.einsum('bld,de->ble', h, w_in)
    rq, rk, rv, rg, mq, mk, mv, mo, mi, mf = _split(proj, AB_SPLITS)
    q = _rope(rq.reshape(B, L, RET_HEADS, RET_DK).astype(f32), positions) * (RET_DK ** -0.5)
    k = _rope(rk.reshape(B, L, RET_HEADS, RET_DK).astype(f32), positions)
    v = rv.reshape(B, L, RET_HEADS, RET_DV).astype(f32)
    o_ret, ret_new = _retention(q, k, v, ret_s.astype(f32))
    o_ret = jax.nn.silu(rg.astype(f32)) * _head_norm(o_ret, ret_gn, True)
    qk, conv_new = _causal_conv(jnp.concatenate([mq, mk], axis=-1), conv_s, conv_w, conv_b)
    qk = jax.nn.silu(qk.astype(f32))
    q_m = qk[..., :ML_HEADS * ML_DK].reshape(B, L, ML_HEADS, ML_DK)
    k_m = qk[..., ML_HEADS * ML_DK:].reshape(B, L, ML_HEADS, ML_DK) * (ML_DK ** -0.5)
    v_m = mv.astype(f32).reshape(B, L, ML_HEADS, ML_DV)
    i_pre = (mi + b_gates[:ML_HEADS]).astype(f32)
    log_f = jax.nn.log_sigmoid((mf + b_gates[ML_HEADS:]).astype(f32))
    h_m, c_new, n_new, m_new = _mlstm(q_m, k_m, v_m, i_pre, log_f,
                                      mc_s.astype(f32), mn_s.astype(f32), mm_s.astype(f32))
    h_m = jax.nn.sigmoid(mo.astype(f32)).reshape(B, L, ML_HEADS, ML_DV) * h_m
    h_m = _head_norm(h_m, ml_gn, True)
    out = jnp.einsum('ble,ed->bld', jnp.concatenate([o_ret, h_m], axis=-1).astype(h.dtype), w_out)
    return out, ret_new, c_new, n_new, m_new, conv_new

def _mixer_c(h, hg_s, lower_bound, w_in, hg_gn, w_out):
    f32 = jnp.float32
    B, L, _ = h.shape
    qp, fp, ip, gp = _split(jnp.einsum('bld,de->ble', h, w_in), C_SPLITS)
    f = lower_bound + (1.0 - lower_bound) * jax.nn.sigmoid(fp.astype(f32))
    shp = (B, L, HG_HEADS, HG_DK)
    q = jax.nn.silu(qp.astype(f32)).reshape(shp)
    k = (1.0 - f).reshape(shp)
    log_f = jnp.log(f).reshape(shp)
    v = ip.astype(f32).reshape(B, L, HG_HEADS, HG_DV)
    o, s_new = _hgrn2(q, k, log_f, v, hg_s.astype(f32))
    o = _head_norm(o, hg_gn, False) * jax.nn.silu(gp.astype(f32))
    return jnp.einsum('ble,ed->bld', o.astype(h.dtype), w_out), s_new

def _swiglu(h, wg, wu, wd):
    a = jnp.einsum('bld,df->blf', h, wg)
    u = jnp.einsum('bld,df->blf', h, wu)
    return jnp.einsum('blf,fd->bld', jax.nn.silu(a) * u, wd)

def _moe(h, w_router, b_router, wg, wu, wd):
    f32 = jnp.float32
    logits = jnp.einsum('bld,de->ble', h, w_router).astype(f32) + b_router.astype(f32)
    top_val, top_idx = lax.top_k(logits, TOP_K)
    top_w = jax.nn.softmax(top_val, axis=-1)
    gates = jnp.sum(jax.nn.one_hot(top_idx, N_EXPERTS, dtype=f32) * top_w[..., None], axis=-2)
    out = jnp.zeros(h.shape, f32)
    for e in range(N_EXPERTS):
        out = out + gates[..., e:e + 1] * _swiglu(h, wg[e], wu[e], wd[e]).astype(f32)
    return out.astype(h.dtype)

def _trunk(x, positions, ret_s, mc_s, mn_s, mm_s, conv_s, hg_s, p):
    P = jax.nn.softmax(p['hg_lower'].astype(jnp.float32), axis=0)
    lower = jnp.cumsum(P, axis=0) - P[0:1]
    ret_l, mc_l, mn_l, mm_l, cv_l, hg_l = [], [], [], [], [], []
    for l in range(DEPTH):
        j = l // 2
        h = _rmsnorm(x, p['ln_mix'][l])
        if l % 2 == 0:
            mix, r_new, c_new, n_new, m_new, cv_new = _mixer_ab(
                h, positions, ret_s[j], mc_s[j], mn_s[j], mm_s[j], conv_s[j],
                p['w_in_ab'][j], p['b_gates_ab'][j], p['conv_w_ab'][j], p['conv_b_ab'][j],
                p['ret_gn'][j], p['ml_gn'][j], p['w_out_ab'][j])
            ret_l.append(r_new.astype(x.dtype))
            mc_l.append(c_new.astype(x.dtype))
            mn_l.append(n_new.astype(x.dtype))
            mm_l.append(m_new.astype(x.dtype))
            cv_l.append(cv_new.astype(x.dtype))
        else:
            mix, s_new = _mixer_c(h, hg_s[j], lower[l], p['w_in_c'][j], p['hg_gn'][j], p['w_out_c'][j])
            hg_l.append(s_new.astype(x.dtype))
        x = x + mix
        h = _rmsnorm(x, p['ln_ffn'][l])
        if l % 2 == 0:
            ffn = _swiglu(h, p['w_ffn_gate'][j], p['w_ffn_up'][j], p['w_ffn_down'][j])
        else:
            ffn = _moe(h, p['w_router'][j], p['b_router'][j], p['w_moe_gate'][j], p['w_moe_up'][j], p['w_moe_down'][j])
        x = x + ffn
    y = _rmsnorm(x, p['ln_final'])
    return (y, jnp.stack(ret_l), jnp.stack(mc_l), jnp.stack(mn_l), jnp.stack(mm_l), jnp.stack(cv_l), jnp.stack(hg_l))

def setup_inputs(seed: int = 0) -> dict:
    key = jax.random.key(seed)
    keys = jax.random.split(key, 32)
    f32 = jnp.float32

    def nrm(i, shape, scale):
        return scale * jax.random.normal(keys[i], shape, f32)

    d = D_MODEL
    qk_w = 2 * ML_HEADS * ML_DK
    return {
        'x_prompt': nrm(0, (BATCH, SEQ, d), 1.0),
        'x_sample': nrm(1, (DEC_BATCH, DEC_SEQ, d), 1.0),
        'state_ret': nrm(2, (N_EVEN, DEC_BATCH, RET_HEADS, RET_DK, RET_DV), 0.5),
        'state_mlstm_c': nrm(3, (N_EVEN, DEC_BATCH, ML_HEADS, ML_DK, ML_DV), 1.0),
        'state_mlstm_n': nrm(4, (N_EVEN, DEC_BATCH, ML_HEADS, ML_DK), 1.0),
        'state_mlstm_m': 2.0 + nrm(5, (N_EVEN, DEC_BATCH, ML_HEADS), 1.0),
        'state_conv': nrm(6, (N_EVEN, DEC_BATCH, ML_CONV - 1, qk_w), 1.0),
        'state_hgrn': nrm(7, (N_ODD, DEC_BATCH, HG_HEADS, HG_DK, HG_DV), 0.5),
        'ln_mix': 1.0 + nrm(8, (DEPTH, d), 0.05),
        'ln_ffn': 1.0 + nrm(9, (DEPTH, d), 0.05),
        'ln_final': 1.0 + nrm(10, (d,), 0.05),
        'w_in_ab': nrm(11, (N_EVEN, d, AB_IN), d ** -0.5),
        'b_gates_ab': jnp.concatenate([nrm(12, (N_EVEN, ML_HEADS), 0.1),
                                       jnp.linspace(FORGET_BIAS_LO, FORGET_BIAS_HI, ML_HEADS, dtype=f32)[None, :]
                                       + nrm(13, (N_EVEN, ML_HEADS), 0.1)], axis=-1),
        'conv_w_ab': nrm(14, (N_EVEN, ML_CONV, qk_w), ML_CONV ** -0.5),
        'conv_b_ab': nrm(15, (N_EVEN, qk_w), 0.02),
        'ret_gn': 1.0 + nrm(16, (N_EVEN, RET_W), 0.05),
        'ml_gn': 1.0 + nrm(17, (N_EVEN, ML_W), 0.05),
        'w_out_ab': nrm(18, (N_EVEN, RET_W + ML_W, d), (RET_W + ML_W) ** -0.5),
        'w_in_c': nrm(19, (N_ODD, d, C_IN), d ** -0.5),
        'hg_lower': 1.0 + nrm(20, (DEPTH, HG_HEADS * HG_DK), 0.1),
        'hg_gn': 1.0 + nrm(21, (N_ODD, HG_W), 0.05),
        'w_out_c': nrm(22, (N_ODD, HG_W, d), HG_W ** -0.5),
        'w_ffn_gate': nrm(23, (N_EVEN, d, D_FF), d ** -0.5),
        'w_ffn_up': nrm(24, (N_EVEN, d, D_FF), d ** -0.5),
        'w_ffn_down': nrm(25, (N_EVEN, D_FF, d), D_FF ** -0.5),
        'w_router': nrm(26, (N_ODD, d, N_EXPERTS), d ** -0.5),
        'b_router': nrm(27, (N_ODD, N_EXPERTS), 0.01),
        'w_moe_gate': nrm(28, (N_ODD, N_EXPERTS, d, D_FF_EXPERT), d ** -0.5),
        'w_moe_up': nrm(29, (N_ODD, N_EXPERTS, d, D_FF_EXPERT), d ** -0.5),
        'w_moe_down': nrm(30, (N_ODD, N_EXPERTS, D_FF_EXPERT, d), D_FF_EXPERT ** -0.5),
    }

def reference(x_prompt, x_sample, state_ret, state_mlstm_c, state_mlstm_n, state_mlstm_m, state_conv, state_hgrn,
              ln_mix, ln_ffn, ln_final, w_in_ab, b_gates_ab, conv_w_ab, conv_b_ab, ret_gn, ml_gn, w_out_ab,
              w_in_c, hg_lower, hg_gn, w_out_c, w_ffn_gate, w_ffn_up, w_ffn_down,
              w_router, b_router, w_moe_gate, w_moe_up, w_moe_down):
    p = {'ln_mix': ln_mix, 'ln_ffn': ln_ffn, 'ln_final': ln_final,
         'w_in_ab': w_in_ab, 'b_gates_ab': b_gates_ab, 'conv_w_ab': conv_w_ab, 'conv_b_ab': conv_b_ab,
         'ret_gn': ret_gn, 'ml_gn': ml_gn, 'w_out_ab': w_out_ab,
         'w_in_c': w_in_c, 'hg_lower': hg_lower, 'hg_gn': hg_gn, 'w_out_c': w_out_c,
         'w_ffn_gate': w_ffn_gate, 'w_ffn_up': w_ffn_up, 'w_ffn_down': w_ffn_down,
         'w_router': w_router, 'b_router': b_router,
         'w_moe_gate': w_moe_gate, 'w_moe_up': w_moe_up, 'w_moe_down': w_moe_down}
    bp, lp = x_prompt.shape[0], x_prompt.shape[1]
    dt = x_prompt.dtype
    (y_prompt, ret_p, mc_p, mn_p, mm_p, conv_p, hg_p) = _trunk(
        x_prompt, jnp.arange(lp, dtype=jnp.int32),
        jnp.zeros((N_EVEN, bp, RET_HEADS, RET_DK, RET_DV), dt),
        jnp.zeros((N_EVEN, bp, ML_HEADS, ML_DK, ML_DV), dt),
        jnp.zeros((N_EVEN, bp, ML_HEADS, ML_DK), dt),
        jnp.full((N_EVEN, bp, ML_HEADS), -jnp.inf, dt),
        jnp.zeros((N_EVEN, bp, ML_CONV - 1, 2 * ML_HEADS * ML_DK), dt),
        jnp.zeros((N_ODD, bp, HG_HEADS, HG_DK, HG_DV), dt),
        p)
    (y_sample, ret_s, mc_s, mn_s, mm_s, conv_s, hg_s) = _trunk(
        x_sample, PAST_LEN + jnp.arange(x_sample.shape[1], dtype=jnp.int32),
        state_ret, state_mlstm_c, state_mlstm_n, state_mlstm_m, state_conv, state_hgrn, p)
    return (y_prompt, y_sample, ret_p, ret_s, mc_p, mc_s, mn_p, mn_s, mm_p, mm_s, conv_p, conv_s, hg_p, hg_s)


_drawn_inputs = setup_inputs


def setup_inputs(seed=0):
    import zlib

    import numpy as np

    out = dict(_drawn_inputs(seed))
    spreads = {}
    factors = {'b_router': 3.045}
    for name, (base, spread) in spreads.items():
        noise = np.random.default_rng([zlib.crc32(name.encode()), seed]).standard_normal(out[name].shape)
        drawn = base * np.exp(spread * noise) if base else spread * noise
        out[name] = jnp.asarray(drawn.astype(out[name].dtype))
    for name, factor in factors.items():
        out[name] = (out[name] * factor).astype(out[name].dtype)
    return out
```

```python
import math
from contextlib import ExitStack

import numpy as np

import concourse.bass as bass
from concourse import mybir

F32 = mybir.dt.float32
I32 = mybir.dt.int32
ALU = mybir.AluOpType
ACT = mybir.ActivationFunctionType
AX = mybir.AxisListType

P = 128
D = 1024
KD = D // P
TP = 256
NB, TS = 8, 8
SMP = NB * TS
NT = TP + SMP
BLK = [(0, 128), (128, 128), (256, 64)]
H4 = 4
HG = 8
DH = 128
FF = 2816
FT = FF // P
NE = 8
PAST = 2048
EPS = 1e-6
NCONV = 4
XW = 3 + TP + NB * (3 + TS)
CW = XW - 3
SX = 3 + TP
FC = 256
NFC = FF // FC
RING = 3
SLOT = 4096
NST = 3
DRING = 3
CAP = 128
BIG = 1024.0
GAMMA = [1.0 - 2.0 ** (-5.0 - h) for h in range(H4)]

CONST = {}
_at = 0
for _name, _width in (("ident", P), ("ones", P), ("inv_d", P), ("inv_h", P), ("center", P),
                      ("cos", NT), ("sin", NT), ("decay", H4 * 320), ("qdec", H4 * SMP), ("kdec", 3 * H4),
                      ("mmask", 192), ("reset", NT), ("minrow", NT), ("level", 7 * P), ("sel", H4 * P),
                      ("bmask", NB), ("slots", CAP), ("tri", P), ("tie", 64), ("eps", 1)):
    CONST[_name] = (_at, _width)
    _at += _width
NCONST = _at

PRM = {}
_at = 0
for _name, _rows in (("ln_mix", 16), ("ln_ffn", 16), ("ln_final", 8), ("conv_w", 32), ("conv_b", 8),
                     ("ret_gn", 4), ("ml_gn", 4), ("hg_lower", 16), ("hg_gn", 8)):
    PRM[_name] = _at
    _at += _rows
NPRM = _at


def constants():
    c = np.zeros((P, NCONST), np.float32)

    def put(name, value):
        a, w = CONST[name]
        value = np.asarray(value, np.float64).reshape(len(value), w)
        c[:len(value), a:a + w] = value.astype(np.float32)

    p = np.arange(P)
    put("ident", np.eye(P))
    put("ones", np.ones((P, P)))
    put("inv_d", np.full((P, P), 1.0 / D))
    put("inv_h", np.full((P, P), 1.0 / DH))
    put("center", np.eye(P) - 1.0 / DH)
    half = DH // 2
    inv = (10000.0 ** (-(np.arange(half, dtype=np.float32) / np.float32(half)).astype(np.float64))).astype(np.float32)
    pos = np.concatenate([np.arange(TP), PAST + np.tile(np.arange(TS), NB)]).astype(np.float32)
    ang = (pos[None, :] * inv[:, None]).astype(np.float32).astype(np.float64)
    put("cos", np.concatenate([np.cos(ang), np.cos(ang)]))
    put("sin", np.concatenate([np.sin(ang), -np.sin(ang)]))
    scale = DH ** -0.5
    s, t = p[:, None], np.arange(TP)[None, :]
    s8, t8 = np.arange(SMP)[:, None], np.arange(SMP)[None, :]
    same = (s8 // TS == t8 // TS) & (t8 >= s8)
    decay = np.zeros((P, H4, 320))
    qdec = np.zeros((P, H4, SMP))
    kdec = np.zeros((P, 3, H4))
    for h, g in enumerate(GAMMA):
        decay[:, h, :TP] = np.where(t >= s, g ** np.maximum(t - s, 0), 0) * scale
        decay[:SMP, h, TP:] = np.where(same, g ** np.maximum(t8 - s8, 0), 0) * scale
        qdec[:, h, :] = (g ** (np.arange(SMP) % TS + 1.0))[None, :] * scale
        kdec[:, 0, h] = g ** (TP - 1.0 - p)
        kdec[:, 1, h] = g ** (TP - 1.0 - P - p)
        kdec[:SMP, 2, h] = g ** (TS - 1.0 - np.arange(SMP) % TS)
    put("decay", decay)
    put("qdec", qdec)
    put("kdec", kdec)
    mmask = np.zeros((P, 192))
    mmask[:, :P] = np.where(p[None, :] >= s, 0, -1e30)
    mmask[:SMP, P:] = np.where(same, 0, -1e30)
    put("mmask", mmask)
    start = np.zeros(NT, bool)
    start[0] = True
    start[TP::TS] = True
    put("reset", np.tile(np.where(start, 0.0, 1.0), (P, 1)))
    put("minrow", np.tile(np.where(start, -3e38, 3e38), (P, 1)))
    level = np.zeros((P, 7, P))
    for j in range(7):
        m = 1 << j
        level[:, j, :] = (s // (2 * m) == p[None, :] // (2 * m)) & (s % (2 * m) < m) & (p[None, :] % (2 * m) >= m)
    put("level", level)
    sel = np.zeros((H4, H4, P))
    for h in range(H4):
        sel[h, h] = 1
    put("sel", sel)
    put("bmask", (np.arange(SMP)[:, None] // TS == np.arange(NB)[None, :]))
    put("slots", np.tile(np.arange(CAP), (P, 1)))
    put("tri", s < p[None, :])
    e = np.arange(NE)
    put("tie", np.tile((e[None, :] < e[:, None]).reshape(1, 64), (P, 1)))
    put("eps", np.full((P, 1), EPS))
    return c


def trunk_kernel(nc, A, O):
    with ExitStack() as ctx:
        def sb(name, shape, dt=F32):
            return ctx.enter_context(nc.sbuf_tensor(name, shape, dt))

        sems = {}

        def S(name):
            if name not in sems:
                sems[name] = ctx.enter_context(nc.semaphore(name))
            return sems[name]

        banks = [ctx.enter_context(nc.psum_tensor(f"bank{i}", [P, 512], F32)) for i in range(8)]

        cst = sb("cst", [P, NCONST])
        ring = sb("ring", [P, RING * SLOT])
        xT = sb("xT", [P, KD, NT])
        hT = sb("hT", [P, KD, NT])
        arena = sb("arena", [P, 26880])
        prm = sb("prm", [P, NPRM])
        wgate = sb("wgate", [P, KD, 2 * H4])
        wrt = sb("wrt", [P, KD, NE])
        brt = sb("brt", [1, NE])
        gbias = sb("gbias", [H4, 2])
        mrow = sb("mrow", [H4, NB])
        small = sb("small", [P, 512])

        def C(name, rows=P):
            a, w = CONST[name]
            return cst[0:rows, a:a + w]

        def prow(name, k):
            return prm[:, PRM[name] + k:PRM[name] + k + 1]

        ident = C("ident")
        ones = C("ones")

        def region(at, *shape):
            n = math.prod(shape)
            v = arena[:, at:at + n]
            if len(shape) == 1:
                return v
            if len(shape) == 2:
                return v.rearrange("p (a b) -> p a b", b=shape[1])
            return v.rearrange("p (a b c) -> p a b c", b=shape[1], c=shape[2])

        Q = region(0, KD, NT)
        K = region(2560, KD, NT)
        G = region(5120, KD, NT)
        V = region(7680, 3, D)
        ST = region(10752, NST, NB, DH)
        KN = region(13824, 2, 3, DH)
        VX = region(14592, NB, DH)
        XC = region(15616, KD, XW)
        CV = region(18392, KD, CW)
        PB = region(21168, 2, 448)
        OR = region(22064, KD, NT)
        WB = region(24624, 448)
        EM = region(25072, 2, NT)
        ROW = region(25712, 3, NT)
        RS = region(15616, KD, NT)
        SQ = region(18392, 2, NT)
        ROT = region(22064, H4, NT)
        CUM = region(15616, KD, NT)
        LV = [region(18176, KD, NT), region(20736, KD, NT)]
        PH = region(23296, HG, 448)
        OH = region(20736, KD, NT)
        XN = region(0, 3, D)
        PN = region(3072, P)
        CN = region(3200, D)
        NN = region(4224, P)
        CT = region(24624, KD, 27)
        CO = arena[0:27, 19152:19152 + D]
        FT_A = region(0, FT, NT)
        SG = region(7040, 2, NT)
        SQF = region(7680, KD, NT)
        HN = region(0, 3, D)
        XG = region(3072, KD, CAP)
        Y = region(4096, D)
        AN = region(5120, 2, FC)
        AT = region(5632, 2, FC)
        SL = region(6144, 2, FC)
        STE = region(6656, NT)
        SE = region(6976, 3, CAP)
        SGE = region(7360, 3, CAP)
        WD = region(10752, DRING, 2048)
        YN = region(15616, 3, D)

        SRC = small[:, 0:24].rearrange("p (c r h) -> p c r h", c=3, r=2)
        NS0 = small[:, 24:56]
        NRAW = small[:, 56:92].rearrange("p (h n) -> p h n", n=9)
        NOUT = small[:, 92:128]
        LB = small[:, 128:136]
        OMLB = small[:, 136:144]
        LBT = small[:, 144:168].rearrange("p (a b) -> p a b", b=8)
        QE = small[:, 168:296].rearrange("p (a b) -> p a b", b=SMP)
        WPS = small[:, 296:424].rearrange("p (a b) -> p a b", b=SMP)
        rows = sb("rows", [H4, 6, NT])
        I_R, B_R, SRC_R, NGM_R, MT_R, WE_R = [rows[:, i, :] for i in range(6)]
        Z_R, L_R, T_R = [ROW[0:H4, i, :] for i in range(3)]
        wprow = sb("wprow", [H4, SMP])
        SPO = sb("SPO", [P, 2, DH])
        ES = C("decay")[:, 0:HG * SMP].rearrange("p (h n) -> p h n", n=SMP)
        NTO = region(24624 + 0, P)[0:36]
        LG = region(8192, 3, NE)
        CMP = region(8216, 3, 64)
        CM2 = region(8408, 3, 64)
        SELM = region(8600, 3, NE)
        GATE = region(8624, 3, NE)
        RANK = region(8648, 3, NE)
        V1 = sb("V1", [P, 3])
        RND = sb("RND", [P, 4])
        NIT = sb("NIT", [1, 1], I32)
        rsq = sb("rsq", [P, NT])
        MDEC = sb("MDEC", [P, 2, NB])

        slots = [ring[:, i * SLOT:(i + 1) * SLOT] for i in range(RING)]

        w_ab = A["w_in_ab"][0].rearrange("(k p) n -> p k n", p=P)
        w_oab = A["w_out_ab"][0].rearrange("(k p) n -> p k n", p=P)
        w_c = A["w_in_c"][0].rearrange("(k p) n -> p k n", p=P)
        w_oc = A["w_out_c"][0].rearrange("(k p) n -> p k n", p=P)
        w_fg = A["w_ffn_gate"][0].rearrange("(k p) n -> p k n", p=P)
        w_fu = A["w_ffn_up"][0].rearrange("(k p) n -> p k n", p=P)
        w_fd = A["w_ffn_down"][0].rearrange("(k p) n -> p k n", p=P)
        AB_ORDER = [4, 5, 6, 0, 1, 2, 3, 7]
        C_ORDER = [2, 3, 0, 1, 4, 5, 6, 7]
        plan = ([("ab", c) for c in AB_ORDER] + [("oab", c) for c in range(2)] + [("ffn", c) for c in range(NFC)]
                + [("fd", c) for c in range(KD)] + [("c", c) for c in C_ORDER] + [("oc", c) for c in range(2)])
        NDENSE = len(plan)
        place = {key: n for n, key in enumerate(plan)}
        dense_uses = [len(range(s, NDENSE, RING)) for s in range(RING)]
        gu_uses = [len(range(s, NFC, RING)) for s in range(RING)]
        d_uses = [len(range(s, NFC, DRING)) for s in range(DRING)]
        last_dense = [max(range(s, NDENSE, RING)) for s in range(RING)]
        w_landed = [S(f"weights_landed_{s}") for s in range(RING)]
        d_landed = [S(f"down_landed_{s}") for s in range(DRING)]

        def chunk_view(key):
            n = place[key]
            slot = slots[n % RING]
            if key[0] == "fd":
                return slot[:, 0:FT * P].rearrange("p (k n) -> p k n", n=P)
            return slot.rearrange("p (k n) -> p k n", n=512)

        filled = {"act": S("filled_for_act"), "dve": S("filled_for_dve")}
        emptied = {"act": S("emptied_by_act"), "dve": S("emptied_by_dve")}
        count = {"act": 0, "dve": 0}
        ticket = {}
        chunk_read = {}

        def bank_of(kind, n):
            return banks[(0 if kind == "act" else 4) + n % 4]

        def after_fill(eng, name):
            kind, n = ticket[name]
            eng.wait_ge(filled[kind], n + 1)

        def after_empty(eng, name):
            kind, n = ticket[name]
            eng.wait_ge(emptied[kind], n + 1)

        def halves(X, j):
            m = 1 << j
            if j >= 3:
                w = X[:, :, 0:TP]
                if j == 7:
                    return w[:, :, 0:P], w[:, :, P:TP], w[:, :, P - 1:P]
                w = w.rearrange("p h (n m) -> p h n m", m=2 * m)
                return w[:, :, :, 0:m], w[:, :, :, m:2 * m], w[:, :, :, m - 1:m]
            w = X.rearrange("p h (n m) -> p (h n) m", m=2 * m)
            return w[:, :, 0:m], w[:, :, m:2 * m], w[:, :, m - 1:m]

        block = ctx.enter_context(nc.Block())

        @block.tensor
        def _(pe):
            mm = nc.tensor.matmul

            def open_bank(kind):
                n = count[kind]
                if n >= 4:
                    pe.wait_ge(emptied[kind], n - 3)
                return bank_of(kind, n)

            def close_bank(kind, ins, name):
                assert name not in ticket
                ticket[name] = (kind, count[kind])
                count[kind] += 1
                ins.then_inc(filled[kind], 1)

            def need_chunk(key):
                n = place[key]
                pe.wait_ge(w_landed[n % RING], 32 * (n // RING + 1))
                return chunk_view(key)

            def read_chunk(key, kind, name):
                chunk_read[place[key]] = (kind, ticket[name][1])

            def gemm_tile(w, cols, src, kind, name, ks, ready=None):
                b = open_bank(kind)
                for k in range(ks):
                    if ready is not None:
                        pe.wait_ge(S(ready), k + 1)
                    ins = mm(b[:, 0:NT], w[:, k, cols:cols + P], src[:, k, :], start=(k == 0), stop=(k == ks - 1))
                close_bank(kind, ins, name)

            def token_tiles(w, key, tag):
                for i, (t0, tn) in enumerate(BLK):
                    b = open_bank("dve")
                    for k in range(KD):
                        ins = mm(b[0:tn, :], hT[:, k, t0:t0 + tn], w[:, k, :], start=(k == 0), stop=(k == KD - 1))
                    close_bank("dve", ins, (tag, i))
                read_chunk(key, "dve", (tag, 2))

            def rms(tag):
                b = open_bank("act")
                for k in range(KD):
                    pe.wait_ge(S(tag + "_squares"), k + 1)
                    ins = mm(b[:, 0:NT], C("inv_d"), SQF[:, k, :], start=(k == 0), stop=(k == KD - 1))
                close_bank("act", ins, (tag, "ms"))

            def head_norm(src, tag, centered):
                for u in range(KD + 1):
                    if u < KD:
                        if centered and u >= H4:
                            pe.wait_ge(S("o_mlstm"), u - H4 + 1)
                        else:
                            after_empty(pe, ("num", 0 if centered else 1, u))
                        b = open_bank("act")
                        ins = mm(b[:, 0:NT], C("center") if centered else ident, src[:, u, :], start=True, stop=True)
                        close_bank("act", ins, (tag, "cen", u))
                    if u > 0:
                        b = open_bank("act")
                        pe.wait_ge(emptied["act"], ticket[(tag, "cen", u - 1)][1] + 1)
                        ins = mm(b[:, 0:NT], C("inv_h"), SQ[:, (u - 1) % 2, :], start=True, stop=True)
                        close_bank("act", ins, (tag, "var", u - 1))

            pe.wait_ge(S("const_in"), 16)
            pe.wait_ge(S("x_in"), 32)
            for k in range(KD):
                b = open_bank("dve")
                for i, (t0, tn) in enumerate(BLK):
                    ins = nc.tensor.transpose(b[:, t0:t0 + tn], XN[0:tn, i, k * P:(k + 1) * P], ident[0:tn, 0:tn])
                close_bank("dve", ins, ("xT", k))
            pe.wait_ge(S("prm_in"), 16 * 9)
            b = open_bank("act")
            ins = nc.tensor.transpose(b[:, 0:NPRM], PN[0:NPRM, :], ident[0:NPRM, 0:NPRM])
            close_bank("act", ins, "prm")
            pe.wait_ge(S("carry_in"), 32)
            b = open_bank("act")
            for k in range(KD):
                nc.tensor.transpose(b[:, 24 * k:24 * k + 24], CN[0:24, k * P:(k + 1) * P], ident[0:24, 0:24])
            ins = nc.tensor.transpose(b[:, 192:224], NN[0:32, :], ident[0:32, 0:32])
            close_bank("act", ins, "carry")

            rms("n0")
            for c in AB_ORDER:
                w = need_chunk(("ab", c))
                if c in (2, 6):
                    token_tiles(w, ("ab", c), ("V", 0, c // 6))
                else:
                    for h in range(H4):
                        gemm_tile(w, h * P, hT, "act", ("ab", c, h), KD, "n0_h" if c == AB_ORDER[0] and h == 0 else None)
                    read_chunk(("ab", c), "act", ("ab", c, H4 - 1))
                if c == 5:
                    pe.wait_ge(S("wgate_in"), 16)
                    for r in range(2):
                        b = open_bank("act")
                        for k in range(KD):
                            ins = mm(b[0:H4, 0:NT], wgate[:, k, r * H4:(r + 1) * H4], hT[:, k, :],
                                     start=(k == 0), stop=(k == KD - 1))
                        close_bank("act", ins, ("gate", r))
            pe.wait_ge(S("gate_exps"), 2)
            b = open_bank("act")
            for i, (t0, tn) in enumerate(BLK):
                for r, row in enumerate((SRC_R, WE_R)):
                    ins = nc.tensor.transpose(b[0:tn, 8 * i + 4 * r:8 * i + 4 * r + 4], row[:, t0:t0 + tn],
                                              ident[0:H4, 0:H4])
            close_bank("act", ins, "cols")
            pe.wait_ge(S("conv_tail"), 1)
            for g in range(2):
                b = open_bank("act")
                for k in range(4):
                    ins = nc.tensor.transpose(b[0:27, k * P:(k + 1) * P], CT[:, 4 * g + k, :], ident)
                close_bank("act", ins, ("conv_out", g))

            def scores(u):
                b = open_bank("dve")
                mm(b[:, 0:TP], K[:, u, 0:P], Q[:, u, 0:TP], start=True, stop=True)
                mm(b[:, TP:TP + P], K[:, u, P:TP], Q[:, u, P:TP], start=True, stop=True)
                ins = mm(b[0:SMP, 384:448], K[:, u, TP:NT], Q[:, u, TP:NT], start=True, stop=True)
                close_bank("dve", ins, ("sc", 0, u))

            def turn_keys(layer, u):
                b = open_bank("act")
                for i, (t0, tn) in enumerate(BLK):
                    ins = nc.tensor.transpose(b[0:tn, i * P:(i + 1) * P], K[:, u, t0:t0 + tn], ident)
                close_bank("act", ins, ("kn", layer, u))

            def weigh(b, left, probs, right, states):
                mm(b[:, 0:TP], left(0), probs[:, 0:TP], start=True, stop=False, skip_group_check=True)
                mm(b[:, P:TP], left(1), probs[:, TP:TP + P], start=False, stop=False, skip_group_check=True)
                ins = mm(b[:, TP:NT], left(2), probs[0:SMP, 384:448], start=False, stop=False, skip_group_check=True)
                if states is None:
                    return mm(b[:, TP:NT], ones, right, start=False, stop=True, skip_group_check=True)
                for s in range(NB):
                    ins = mm(b[:, TP + s * TS:TP + (s + 1) * TS], states[:, s, :], right[:, s * TS:(s + 1) * TS],
                             start=False, stop=(s == NB - 1), skip_group_check=True)
                return ins

            def outputs(layer, u, probs, probs_ready, right):
                values = lambda i: V[0:BLK[i][1], i, u * DH:(u + 1) * DH]
                probs_ready()
                pe.wait_ge(S(f"qe{layer}"), u + 1)
                pe.wait_ge(S(f"state_in_{layer}_{u % NST}"), 16 * (u // NST + 1))
                b = open_bank("dve")
                ins = weigh(b, values, probs, right, ST[:, u % NST])
                close_bank("dve", ins, ("num", layer, u))
                if layer == 0 and u >= H4:
                    b = open_bank("dve")
                    pe.wait_ge(S("qn"), u - H4 + 1)
                    ins = weigh(b, lambda i: ones[0:BLK[i][1], :], probs, WPS[:, u % 2, :], None)
                    close_bank("dve", ins, ("den", u))

            def state(layer, u):
                after_empty(pe, ("kn", layer, u))
                kn = KN[:, u % 2]
                v = lambda i: V[0:BLK[i][1], i, u * DH:(u + 1) * DH]
                b = open_bank("act")
                mm(b[:, 0:DH], kn[:, 0, :], v(0), start=True, stop=False)
                ins = mm(b[:, 0:DH], kn[:, 1, :], v(1), start=False, stop=True)
                if layer == 0 and u >= H4:
                    mm(b[:, DH:DH + 1], kn[:, 0, :], ones[:, 0:1], start=True, stop=False)
                    mm(b[:, DH:DH + 1], kn[:, 1, :], ones[:, 0:1], start=False, stop=True)
                    ins = mm(b[:, DH + 1:DH + 9], kn[0:SMP, 2, :], C("bmask", SMP), start=True, stop=True)
                close_bank("act", ins, ("sp", layer, u))
                pe.wait_ge(S(f"vx{layer}"), u + 1)
                for g in range(2):
                    b = open_bank("dve")
                    ins = mm(b[:, :].rearrange("p (b v) -> p b v", v=DH), kn[0:SMP, 2, :],
                             VX[0:SMP, 4 * g:4 * g + 4, :], start=True, stop=True)
                    close_bank("dve", ins, ("ss", layer, u, g))

            pe.wait_ge(S("rope_done"), 2)
            for u in range(KD + 1):
                if H4 <= u < KD:
                    h = u - H4
                    sel = C("sel", H4).rearrange("r (h p) -> r h p", p=P)[:, h, :]
                    b = open_bank("dve")
                    mm(b[:, 0:NT], sel, NGM_R, start=True, stop=True)
                    ins = mm(b[:, NT:NT + SMP], sel, wprow[:, :], start=True, stop=True)
                    close_bank("dve", ins, ("bc", u))
                    b = open_bank("act")
                    ins = mm(b[:, 0:NT], sel, MT_R, start=True, stop=True)
                    close_bank("act", ins, ("em", u))
                if u > 0:
                    outputs(0, u - 1, PB[:, (u - 1) % 2, :], lambda: after_empty(pe, ("sc", 0, u - 1)), QE[:, (u - 1) % 2, :])
                if u < KD:
                    if u == H4:
                        pe.wait_ge(S("keys_scaled"), 1)
                    scores(u)
                    turn_keys(0, u)
                if u > 0:
                    state(0, u - 1)
            pe.wait_ge(S("n_out"), 1)
            b = open_bank("act")
            ins = nc.tensor.transpose(b[0:36, 0:P], NOUT, ident)
            close_bank("act", ins, "n_out")
            head_norm(OR, "hn0", True)
            pe.wait_ge(S("mix0"), KD)

            def projection_out(kind):
                for c in range(2):
                    w = need_chunk((kind, c))
                    for m in range(4):
                        gemm_tile(w, m * P, hT, "dve", (kind, 4 * c + m), KD)
                    read_chunk((kind, c), "dve", (kind, 4 * c + 3))

            projection_out("oab")

            rms("n1")
            for c in range(NFC):
                w = need_chunk(("ffn", c))
                for j in range(2):
                    gemm_tile(w, j * P, hT, "act", ("fg", 2 * c + j), KD, "n1_h" if c == 0 and j == 0 else None)
                    gemm_tile(w, FC + j * P, hT, "dve", ("fu", 2 * c + j), KD)
                read_chunk(("ffn", c), "dve", ("fu", 2 * c + 1))
            after_empty(pe, ("fu", FT - 1))
            for m in range(KD):
                w = need_chunk(("fd", m))
                gemm_tile(w, 0, FT_A, "dve", ("fd", m), FT)
                read_chunk(("fd", m), "dve", ("fd", m))

            rms("n2")
            for c in C_ORDER:
                w = need_chunk(("c", c))
                if c in (4, 5):
                    token_tiles(w, ("c", c), ("V", 1, c - 4))
                else:
                    for h in range(4):
                        gemm_tile(w, h * P, hT, "act", ("c", c, h), KD, "n2_h" if c == C_ORDER[0] and h == 0 else None)
                    read_chunk(("c", c), "act", ("c", c, 3))
            pe.wait_ge(S("hgrn_k"), HG)
            after_empty(pe, ("c", 1, 3))
            for h in range(0, HG, 2):
                b = open_bank("dve")
                for j in range(2):
                    for i in range(2):
                        at = slice(i * P, (i + 1) * P)
                        ins = mm(b[:, (2 * j + i) * P:(2 * j + i + 1) * P], K[:, h + j, at], Q[:, h + j, at],
                                 start=True, stop=True)
                close_bank("dve", ins, ("diag", h))
            b = open_bank("dve")
            for h in range(HG):
                ins = mm(b[0:SMP, h * SMP:(h + 1) * SMP], K[:, h, TP:NT], Q[:, h, TP:NT], start=True, stop=True)
            close_bank("dve", ins, ("diag", "s"))
            for j in range(7, -1, -1):
                L = LV[j % 2]
                pe.wait_ge(S("level_k"), 8 - j)
                pe.wait_ge(S("level_q"), 8 - j)
                if j == 7:
                    for g in range(2):
                        b = open_bank("dve")
                        for h in range(4):
                            ins = mm(b[:, h * P:(h + 1) * P], L[:, 4 * g + h, 0:P], L[:, 4 * g + h, P:TP],
                                     start=True, stop=True)
                        close_bank("dve", ins, ("lv", j, g))
                    continue
                for h in range(0, HG, 2):
                    b = open_bank("dve")
                    for q in range(2):
                        for i in range(2):
                            at = slice(i * P, (i + 1) * P)
                            ins = mm(b[:, (2 * q + i) * P:(2 * q + i + 1) * P], L[:, h + q, at], L[:, h + q, at],
                                     start=True, stop=True)
                    close_bank("dve", ins, ("lv", j, h))
                if j < 3:
                    b = open_bank("dve")
                    for h in range(HG):
                        ins = mm(b[0:SMP, h * SMP:(h + 1) * SMP], L[:, h, TP:NT], L[:, h, TP:NT], start=True, stop=True)
                    close_bank("dve", ins, ("lv", j, "s"))
            pe.wait_ge(S("hgrn_kend"), 1)
            for u in range(HG + 1):
                if u > 0:
                    outputs(1, u - 1, PH[:, u - 1, :], lambda: None, Q[:, u - 1, TP:NT])
                if u < HG:
                    turn_keys(1, u)
                if u > 0:
                    state(1, u - 1)
            head_norm(OH, "hn1", False)
            pe.wait_ge(S("mix1"), KD)
            projection_out("oc")

            rms("n3")
            pe.wait_ge(S("n3_h"), KD)
            pe.wait_ge(S("router_in"), 32)
            b = open_bank("dve")
            for i, (t0, tn) in enumerate(BLK):
                for k in range(KD):
                    mm(b[0:tn, i * NE:(i + 1) * NE], hT[:, k, t0:t0 + tn], wrt[:, k, :], start=(k == 0), stop=False)
                ins = mm(b[0:tn, i * NE:(i + 1) * NE], ones[0:1, 0:tn], brt[:, :], start=False, stop=True)
            close_bank("dve", ins, "logits")
            for i, (t0, tn) in enumerate(BLK):
                for g in range(2):
                    b = open_bank("act")
                    for k in range(4):
                        ins = nc.tensor.transpose(b[0:tn, k * P:(k + 1) * P], hT[:, 4 * g + k, t0:t0 + tn], ident)
                    close_bank("act", ins, ("hn", i, g))
            pe.wait_ge(S("chosen"), 1)
            b = open_bank("dve")
            for i, (t0, tn) in enumerate(BLK):
                for j in range(i):
                    mm(b[0:tn, i * NE:(i + 1) * NE], ones[:, 0:tn], SELM[:, j, :], start=(j == 0), stop=False)
                mm(b[0:tn, i * NE:(i + 1) * NE], C("tri")[0:tn, 0:tn], SELM[0:tn, i, :], start=(i == 0), stop=True)
            for i, (t0, tn) in enumerate(BLK):
                ins = mm(b[:, 3 * NE:4 * NE], ones[0:tn, :], SELM[0:tn, i, :], start=(i == 0), stop=(i == 2))
            close_bank("dve", ins, "ranks")

            after_empty(pe, "ranks")
            after_empty(pe, ("hn", 2, 1))

            def gather():
                for g in range(2):
                    for m in range(4):
                        for i, (t0, tn) in enumerate(BLK):
                            at = (4 * g + m) * P
                            ins = mm(banks[6 + g][:, m * CAP:(m + 1) * CAP], HN[0:tn, i, at:at + P], SE[0:tn, i, :],
                                     start=(i == 0), stop=(i == 2))
                    ins.then_inc(S("misc_full"), 1)

            pe.wait_ge(S("rounds_known"), 1)
            rounds = pe.value_load(NIT[0:1, 0:1], min_val=NE, max_val=3 * NE)
            pe.wait_ge(S("sel_ready"), 1)
            gather()
            with pe.Fori(0, rounds) as it:
                def gate_up(c):
                    s = c % RING
                    pe.wait_ge(w_landed[s], it * (32 * gu_uses[s]) + 32 * (dense_uses[s] + c // RING + 1))
                    if c >= 2:
                        pe.wait_ge(S("a_ready"), it * NFC + c - 1)
                    if c == 0:
                        pe.wait_ge(S("misc_done"), it * 10 + 2)
                    w = slots[s].rearrange("p (k n) -> p k n", n=512)
                    for k in range(KD):
                        ins = mm(banks[c % 2][:, :], XG[:, k, :], w[:, k, :], start=(k == 0), stop=(k == KD - 1))
                    ins.then_inc(S("gu_full"), 1)

                def turn(c):
                    pe.wait_ge(S("a_ready"), it * NFC + c + 1)
                    t = c if c < NFC - 1 else NFC
                    if c >= 2:
                        pe.wait_ge(S("t_copied"), it * 12 + t - 1)
                    for j in range(2):
                        ins = nc.tensor.transpose(banks[4 + t % 2][:, j * P:(j + 1) * P], AN[:, c % 2, j * P:(j + 1) * P],
                                                  ident)
                    ins.then_inc(S("t_full"), 1)

                def turn_selection():
                    t = NFC - 1
                    pe.wait_ge(S("t_copied"), it * 12 + t - 1)
                    for i, (t0, tn) in enumerate(BLK):
                        ins = nc.tensor.transpose(banks[4 + t % 2][:, t0:t0 + tn], SGE[0:tn, i, :], ident[0:tn, 0:tn])
                    ins.then_inc(S("t_full"), 1)

                def down(c):
                    s = c % DRING
                    pe.wait_ge(d_landed[s], it * (16 * d_uses[s]) + 16 * (c // DRING + 1))
                    t = c if c < NFC - 1 else NFC
                    pe.wait_ge(S("t_copied"), it * 12 + t + 1)
                    w = WD[:, s, :].rearrange("p (j n) -> p j n", n=D)
                    for j in range(2):
                        for g in range(2):
                            ins = mm(banks[2 + g][:, :], AT[:, c % 2, j * P:(j + 1) * P], w[:, j, g * 512:(g + 1) * 512],
                                     start=(c == 0 and j == 0), stop=(c == NFC - 1 and j == 1))
                    ins.then_inc(S("down_done"), 1)

                for c in range(NFC):
                    gate_up(c)
                    if c >= 1:
                        turn(c - 1)
                    if c >= 2:
                        down(c - 2)
                pe.wait_ge(S("sel_ready"), it + 2)
                pe.wait_ge(S("misc_done"), it * 10 + 2)
                gather()
                turn_selection()
                turn(NFC - 1)
                down(NFC - 2)
                down(NFC - 1)
                pe.wait_ge(S("y_copied"), it + 1)
                for m in range(KD):
                    pe.wait_ge(S("misc_done"), it * 10 + m + 3)
                    ins = mm(banks[6 + m % 2][:, 0:NT], Y[:, m * P:(m + 1) * P], STE, start=True, stop=True)
                    ins.then_inc(S("misc_full"), 1)

            rms("n4")
            pe.wait_ge(S("n4_h"), KD)
            for i, (t0, tn) in enumerate(BLK):
                for g in range(2):
                    b = open_bank("act")
                    for k in range(4):
                        ins = nc.tensor.transpose(b[0:tn, k * P:(k + 1) * P], hT[:, 4 * g + k, t0:t0 + tn], ident)
                    close_bank("act", ins, ("yn", i, g))

        @block.sync
        def _(sp):
            x_p = A["x_prompt"][0].rearrange("(i p) d -> p i d", p=P)
            x_s = A["x_sample"].rearrange("b t d -> (b t) d")
            sp.dma_start(XN[:, 0:2, :], x_p).then_inc(S("x_in"), 16)
            sp.dma_start(XN[0:SMP, 2, :], x_s).then_inc(S("x_in"), 16)

            def load_dense(n):
                if n >= RING:
                    kind, fill = chunk_read[n - RING]
                    sp.wait_ge(filled[kind], fill + 1)
                key, c = plan[n]
                v = chunk_view(plan[n])
                sem = w_landed[n % RING]
                if key == "ffn":
                    sp.dma_start(v[:, :, 0:FC], w_fg[:, :, c * FC:(c + 1) * FC]).then_inc(sem, 16)
                    sp.dma_start(v[:, :, FC:2 * FC], w_fu[:, :, c * FC:(c + 1) * FC]).then_inc(sem, 16)
                elif key == "fd":
                    src = w_fd[:, :, c * P:(c + 1) * P]
                    sp.dma_start(v[:, 0:FT // 2, :], src[:, 0:FT // 2, :]).then_inc(sem, 16)
                    sp.dma_start(v[:, FT // 2:FT, :], src[:, FT // 2:FT, :]).then_inc(sem, 16)
                else:
                    src = {"ab": w_ab, "oab": w_oab, "c": w_c, "oc": w_oc}[key][:, :, c * 512:(c + 1) * 512]
                    sp.dma_start(v[:, 0:4, :], src[:, 0:4, :]).then_inc(sem, 16)
                    sp.dma_start(v[:, 4:8, :], src[:, 4:8, :]).then_inc(sem, 16)

            for n in range(NDENSE):
                load_dense(n)

            wg = A["w_moe_gate"].rearrange("o e (k p) n -> p (o e) k n", p=P)
            wu = A["w_moe_up"].rearrange("o e (k p) n -> p (o e) k n", p=P)
            wd = A["w_moe_down"].rearrange("o e (k p) n -> p (o e) k n", p=P)

            def load_gate_up(e, c):
                v = slots[c % RING].rearrange("p (k n) -> p k n", n=512)
                sem = w_landed[c % RING]
                for part, w in enumerate((wg, wu)):
                    src = w[:, bass.ds(e, 1), :, c * FC:(c + 1) * FC].rearrange("p o k n -> p (o k) n")
                    sp.dma_start(v[:, :, part * FC:(part + 1) * FC], src).then_inc(sem, 16)

            def load_down(e, c):
                src = wd[:, bass.ds(e, 1), 2 * c:2 * c + 2, :].rearrange("p o k n -> p (o k) n")
                sp.dma_start(WD[:, c % DRING, :].rearrange("p (j n) -> p j n", n=D), src).then_inc(
                    d_landed[c % DRING], 16)

            def load_expert(e, done):
                for c in range(NFC + 2):
                    if c < NFC:
                        if c >= RING:
                            sp.wait_ge(S("gu_full"), c - RING + 1 if done is None else done + (c - RING + 1))
                        elif done is not None:
                            before = max(range(c, NFC, RING))
                            sp.wait_ge(S("gu_full"), done + (before + 1 - NFC))
                        else:
                            kind, fill = chunk_read[last_dense[c]]
                            sp.wait_ge(filled[kind], fill + 1)
                        load_gate_up(e, c)
                    d = c - 2
                    if d >= 0:
                        if d == 0 and done is None:
                            for s in range(NST):
                                sp.wait_ge(S(f"state_out_{s}"), 16 * len(range(s, KD, NST)) * 2)
                        if d >= DRING:
                            sp.wait_ge(S("down_done"), d - DRING + 1 if done is None else done + (d - DRING + 1))
                        elif done is not None:
                            before = max(range(d, NFC, DRING))
                            sp.wait_ge(S("down_done"), done + (before + 1 - NFC))
                        load_down(e, d)

            load_expert(0, None)
            sp.wait_ge(S("rounds_known"), 1)
            rounds = sp.value_load(NIT[0:1, 0:1], min_val=NE, max_val=3 * NE)
            with sp.Fori(1, rounds) as it:
                e = it & (NE - 1)
                sp.compute_val(e)
                load_expert(e, it * NFC)

            y_p = O["y_prompt"][0].rearrange("(i p) d -> p i d", p=P)
            y_s = O["y_sample"].rearrange("b t d -> (b t) d")
            after_empty(sp, ("yn", 1, 1))
            sp.dma_start(y_p, YN[:, 0:2, :]).then_inc(S("y_out"), 16)
            after_empty(sp, ("yn", 2, 1))
            sp.dma_start(y_s, YN[0:SMP, 2, :]).then_inc(S("y_out"), 16)
            sp.wait_ge(S("y_out"), 32)

        @block.scalar
        def _(act):
            tick = {"n": 0}
            act_step = S("act_step")

            def step(ins):
                tick["n"] += 1
                ins.then_inc(act_step, 1)
                return tick["n"]

            def take(name):
                after_fill(act, name)
                kind, n = ticket[name]
                assert kind == "act"
                return bank_of("act", n)

            def free(ins):
                ins.then_inc(emptied["act"], 1)

            fn = nc.scalar.activation

            act.dma_start(cst[:, :], A["cst"]).then_inc(S("const_in"), 16)
            for name, key, nrows in (("ln_mix", "ln_mix", 16), ("ln_ffn", "ln_ffn", 16), ("ln_final", "ln_final", 8),
                                     ("conv_w", "conv_w_ab", 32), ("conv_b", "conv_b_ab", 8), ("ret_gn", "ret_gn", 4),
                                     ("ml_gn", "ml_gn", 4), ("hg_lower", "hg_lower", 16), ("hg_gn", "hg_gn", 8)):
                a = A[key]
                pattern = {1: "(k p) -> k p", 2: "a (k p) -> (a k) p", 3: "o a (k p) -> (o a k) p"}[len(a.shape)]
                act.dma_start(PN[PRM[name]:PRM[name] + nrows, :], a.rearrange(pattern, p=P)).then_inc(S("prm_in"), 16)
            act.dma_start(CN[0:24, :], A["state_conv"][0].rearrange("b j c -> (b j) c")).then_inc(S("carry_in"), 16)
            act.dma_start(NN[0:32, :], A["state_mlstm_n"][0].rearrange("b h k -> (b h) k")).then_inc(S("carry_in"), 16)
            act.dma_start(wgate[:, :, :], w_ab[:, :, 4096:4104]).then_inc(S("wgate_in"), 16)
            act.dma_start(gbias[:, :], A["b_gates_ab"][0].rearrange("(r h) -> h r", r=2),
                          allow_slow_non_contiguous=True).then_inc(S("rows_in"), 16)
            act.dma_start(mrow[:, :], A["state_mlstm_m"][0].rearrange("b h -> h b"),
                          allow_slow_non_contiguous=True).then_inc(S("rows_in"), 16)
            act.dma_start(wrt[:, :, :], A["w_router"][0].rearrange("(k p) e -> p k e", p=P)).then_inc(S("router_in"), 16)
            act.dma_start(brt[:, :], A["b_router"]).then_inc(S("router_in"), 16)

            def squares(tag, ready):
                for k in range(KD):
                    ready(k)
                    fn(SQF[:, k, :], xT[:, k, :], ACT.Square).then_inc(S(tag + "_squares"), 1)

            def root(tag):
                b = take((tag, "ms"))
                free(fn(RSQ, b[:, 0:NT], ACT.Sqrt, bias=C("eps")))

            RSQ = rsq[:, :]

            free(fn(prm[:, :], take("prm")[:, 0:NPRM], ACT.Copy))
            b = take("carry")
            act.wait_ge(S("history_zero"), 1)
            hist = XC[:, :, SX:XW].rearrange("p k (b t) -> p k b t", t=3 + TS)[:, :, :, 0:3]
            for k in range(KD):
                fn(hist[:, k], b[:, 24 * k:24 * k + 24].rearrange("p (b j) -> p b j", j=3), ACT.Copy)
            free(fn(NS0, b[:, 192:224], ACT.Copy))
            squares("n0", lambda k: after_empty(act, ("xT", k)))
            root("n0")
            for c in AB_ORDER:
                if c in (2, 6):
                    continue
                for h in range(H4):
                    b = take(("ab", c, h))
                    if c in (4, 5):
                        k = 4 * (c - 4) + h
                        fn(XC[:, k, 3:SX], b[:, 0:TP], ACT.Copy)
                        new = XC[:, k, SX:XW].rearrange("p (b t) -> p b t", t=3 + TS)[:, :, 3:3 + TS]
                        free(fn(new, b[:, TP:NT].rearrange("p (b t) -> p b t", t=TS), ACT.Copy))
                    elif c in (0, 1):
                        free(fn((Q, K)[c][:, h, :], b[:, 0:NT], ACT.Copy))
                    elif c == 3:
                        free(fn(G[:, h, :], b[:, 0:NT], ACT.Silu))
                    else:
                        free(fn(G[:, H4 + h, :], b[:, 0:NT], ACT.Sigmoid))
                if c == 5:
                    act.wait_ge(S("rows_in"), 32)
                    free(fn(I_R, take(("gate", 0))[0:H4, 0:NT], ACT.Identity, bias=gbias[:, 0:1]))
                    free(fn(Z_R, take(("gate", 1))[0:H4, 0:NT], ACT.Identity, bias=gbias[:, 1:2]))
                    act.wait_ge(S("gate_abs"), 1)
                    n = step(fn(L_R, T_R, ACT.Exp, scale=-1.0))
                    act.wait_ge(act_step, n)
                    fn(L_R, L_R, ACT.Ln, bias=1.0).then_inc(S("gate_ln"), 1)
                    act.wait_ge(S("gate_exps_in"), 1)
                    fn(wprow[:, :], wprow[:, :], ACT.Exp).then_inc(S("gate_exps"), 1)
                    fn(WE_R, WE_R, ACT.Exp).then_inc(S("gate_exps"), 1)
                if c == 0:
                    for k in range(KD):
                        act.wait_ge(S("conv_sum"), k + 1)
                        dst = (Q if k < 4 else K)[:, H4 + k % 4, :]
                        fn(dst[:, 0:TP], CV[:, k, 0:TP], ACT.Silu)
                        for s in range(NB):
                            at = SX + 11 * s
                            ins = fn(dst[:, TP + TS * s:TP + TS * s + TS], CV[:, k, at:at + TS], ACT.Silu)
                        ins.then_inc(S("conv_silu"), 1)
            b = take("cols")
            for i, (t0, tn) in enumerate(BLK):
                ins = fn(SRC[0:tn, i].rearrange("p r h -> p (r h)"), b[0:tn, 8 * i:8 * i + 8], ACT.Copy)
            free(ins)
            for g in range(2):
                free(fn(CO[:, g * 512:(g + 1) * 512], take(("conv_out", g))[0:27, :], ACT.Copy))
            after_empty(act, ("conv_out", 1))
            act.dma_start(O["conv_p"][0, 0], CO[0:3, :]).then_inc(S("stores"), 16)
            act.dma_start(O["conv_s"][0].rearrange("b j c -> (b j) c"), CO[3:27, :]).then_inc(S("stores"), 16)

            def keys(layer, u, scale):
                b = take(("kn", layer, u))
                for i, (t0, tn) in enumerate(BLK):
                    dst, src = KN[0:tn, u % 2, i, :], b[0:tn, i * P:(i + 1) * P]
                    ins = fn(dst, src, ACT.Copy) if scale is None else fn(dst, src, ACT.Copy, scale=scale(i, tn))
                free(ins)

            def prompt_state(layer, u):
                b = take(("sp", layer, u))
                if u + 8 * layer >= 2:
                    act.wait_ge(S(f"sp_stored_{u % 2}"), 16 * ((u + 8 * layer) // 2))
                ins = fn(SPO[:, u % 2, :], b[:, 0:DH], ACT.Copy)
                if layer == 0 and u >= H4:
                    ins = fn(NRAW[:, u - H4, :], b[:, DH:DH + 9], ACT.Copy)
                free(ins)
                out = O["hg_p"] if layer else O["ret_p"] if u < H4 else O["mc_p"]
                after_empty(act, ("sp", layer, u))
                act.dma_start(out[0, 0, u if layer else u % H4], SPO[:, u % 2, :]).then_inc(S(f"sp_stored_{u % 2}"), 16)

            kdec = C("kdec").rearrange("p (i h) -> p i h", h=H4)
            for u in range(KD + 1):
                if H4 <= u < KD:
                    b = take(("em", u))
                    if u >= H4 + 2:
                        after_empty(act, ("den", u - 2))
                    free(fn(EM[:, u % 2, :], b[:, 0:NT], ACT.Exp, scale=-1.0))
                    after_empty(act, ("bc", u))
                    h = u - H4
                    fn(WB[:, 0:TP], WB[:, 0:TP], ACT.Exp, bias=SRC[:, 0, 0, h:h + 1])
                    fn(WB[:, TP:384], WB[:, TP:384], ACT.Exp, bias=SRC[:, 1, 0, h:h + 1])
                    fn(WB[0:SMP, 384:448], WB[0:SMP, 384:448], ACT.Exp,
                       bias=SRC[0:SMP, 2, 0, h:h + 1]).then_inc(S("w_exp"), 1)
                if u < KD:
                    if u < H4:
                        keys(0, u, lambda i, tn: kdec[0:tn, i, u:u + 1])
                    else:
                        keys(0, u, lambda i, tn: SRC[0:tn, i, 1, u - H4:u - H4 + 1])
                if u > 0:
                    prompt_state(0, u - 1)
            free(fn(NTO[:, :], take("n_out")[0:36, 0:P], ACT.Copy))
            after_empty(act, "n_out")
            act.dma_start(O["mn_s"][0].rearrange("b h k -> (b h) k"), NTO[0:32, :]).then_inc(S("stores"), 16)
            act.dma_start(O["mn_p"][0, 0], NTO[32:36, :]).then_inc(S("stores"), 16)
            act.dma_start(O["mm_s"][0].rearrange("b h -> h b"),
                          MT_R[:, TP:NT].rearrange("h (b t) -> h b t", t=TS)[:, :, TS - 1:TS].rearrange("h b o -> h (b o)"),
                          allow_slow_non_contiguous=True).then_inc(S("stores"), 16)
            act.dma_start(O["mm_p"][0].rearrange("b h -> h b"), MT_R[:, TP - 1:TP],
                          allow_slow_non_contiguous=True).then_inc(S("stores"), 16)

            def head_norm(dst, tag):
                for u in range(KD + 1):
                    if u < KD:
                        b = take((tag, "cen", u))
                        if u >= 2:
                            after_fill(act, (tag, "var", u - 2))
                        fn(dst[:, u, :], b[:, 0:NT], ACT.Copy)
                        free(fn(SQ[:, u % 2, :], b[:, 0:NT], ACT.Square))
                    if u > 0:
                        free(fn(RS[:, u - 1, :], take((tag, "var", u - 1))[:, 0:NT], ACT.Sqrt, bias=C("eps")))

            head_norm(OR, "hn0")
            squares("n1", lambda k: after_empty(act, ("oab", k)))
            root("n1")
            for f in range(FT):
                b = take(("fg", f))
                if f >= 2:
                    after_empty(act, ("fu", f - 2))
                free(fn(SG[:, f % 2, :], b[:, 0:NT], ACT.Silu))
            squares("n2", lambda k: after_empty(act, ("fd", k)))
            act.wait_ge(S("lb_max"), 1)
            fn(LBT[:, 0:2, :], LBT[:, 0:2, :], ACT.Exp).then_inc(S("lb_exp"), 1)
            root("n2")
            for c in C_ORDER:
                if c in (4, 5):
                    continue
                for h in range(4):
                    b = take(("c", c, h))
                    if c in (2, 3):
                        free(fn(K[:, 4 * (c - 2) + h, :], b[:, 0:NT], ACT.Sigmoid))
                    elif c in (0, 1):
                        free(fn(Q[:, 4 * c + h, :], b[:, 0:NT], ACT.Silu))
                    else:
                        free(fn(G[:, 4 * (c - 6) + h, :], b[:, 0:NT], ACT.Silu))
            for h in range(HG):
                act.wait_ge(S("forget"), h + 1)
                fn(LV[1][:, h, :], LV[1][:, h, :], ACT.Ln).then_inc(S("forget_ln"), 1)
            for j in range(7, -1, -1):
                act.wait_ge(S("level_diff"), 8 - j)
                L = LV[j % 2]
                cols = slice(0, TP) if j >= 3 else slice(0, NT)
                fn(L[:, :, cols], L[:, :, cols], ACT.Exp).then_inc(S("level_exp"), 1)
            act.wait_ge(S("end_diff"), 1)
            fn(LV[0][:, :, :], LV[0][:, :, :], ACT.Exp).then_inc(S("end_exp"), 1)
            fn(ES[:, :, :], CUM[:, :, TP:NT], ACT.Exp).then_inc(S("end_exp"), 1)
            for u in range(HG + 1):
                if u < HG:
                    keys(1, u, None)
                if u > 0:
                    prompt_state(1, u - 1)
            head_norm(OH, "hn1")
            squares("n3", lambda k: after_empty(act, ("oc", k)))
            root("n3")
            for i, (t0, tn) in enumerate(BLK):
                for g in range(2):
                    free(fn(HN[0:tn, i, g * 512:(g + 1) * 512], take(("hn", i, g))[0:tn, :], ACT.Copy))
            act.wait_ge(S("router_diff"), 1)
            fn(GATE[:, :, :], GATE[:, :, :], ACT.Exp).then_inc(S("router_exp"), 1)

            act.wait_ge(S("rounds_known"), 1)
            rounds = act.value_load(NIT[0:1, 0:1], min_val=NE, max_val=3 * NE)
            with act.Fori(0, rounds) as it:
                def silu(c):
                    act.wait_ge(S("gu_full"), it * NFC + c + 1)
                    if c >= 2:
                        act.wait_ge(S("a_ready"), it * NFC + c - 1)
                    fn(SL[:, c % 2, :], banks[c % 2][:, 0:FC], ACT.Silu).then_inc(S("silu_done"), 1)

                def turned(c):
                    t = c if c < NFC - 1 else NFC
                    act.wait_ge(S("t_full"), it * 12 + t + 1)
                    if c >= 2:
                        act.wait_ge(S("down_done"), it * NFC + c - 1)
                    fn(AT[:, c % 2, :], banks[4 + t % 2][:, 0:FC], ACT.Copy).then_inc(S("t_copied"), 1)

                silu(0)
                for c in range(1, NFC):
                    silu(c)
                    turned(c - 1)
                act.wait_ge(S("t_full"), it * 12 + NFC)
                act.wait_ge(S("misc_full"), it * 10 + 2)
                fn(STE, banks[4][:, 0:NT], ACT.Copy).then_inc(S("t_copied"), 1)
                turned(NFC - 1)
                act.wait_ge(S("down_done"), it * NFC + NFC)
                fn(Y[:, 0:512], banks[2][:, :], ACT.Copy)
                fn(Y[:, 512:1024], banks[3][:, :], ACT.Copy).then_inc(S("y_copied"), 1)

            act.wait_ge(S("misc_done"), rounds * 10 + 2)
            squares("n4", lambda k: None)
            root("n4")
            for i, (t0, tn) in enumerate(BLK):
                for g in range(2):
                    free(fn(YN[0:tn, i, g * 512:(g + 1) * 512], take(("yn", i, g))[0:tn, :], ACT.Copy))
            act.wait_ge(S("stores"), 16 * 6)
            for r in range(2):
                act.wait_ge(S(f"sp_stored_{r}"), 16 * 8)

        @block.vector
        def _(dve):
            tick = {"n": 0}
            dve_step = S("dve_step")
            v = nc.vector

            def step(ins):
                tick["n"] += 1
                ins.then_inc(dve_step, 1)
                dve.wait_ge(dve_step, tick["n"])

            def take(name):
                after_fill(dve, name)
                kind, n = ticket[name]
                assert kind == "dve"
                return bank_of("dve", n)

            def free(ins):
                ins.then_inc(emptied["dve"], 1)

            def normed(tag, gain, row):
                after_empty(dve, (tag, "ms"))
                step(v.reciprocal(rsq[:, :], rsq[:, :]))
                for k in range(KD):
                    v.scalar_tensor_tensor(out=hT[:, k, :], in0=xT[:, k, :], scalar=prow(gain, row + k), in1=rsq[:, :],
                                           op0=ALU.mult, op1=ALU.mult).then_inc(S(tag + "_h"), 1)

            def add_to_x(name, k):
                b = take(name)
                free(v.tensor_tensor(xT[:, k, :], xT[:, k, :], b[:, 0:NT], ALU.add))

            for k in range(KD):
                free(v.tensor_copy(xT[:, k, :], take(("xT", k))[:, 0:NT]))
            after_empty(dve, "prm")
            normed("n0", "ln_mix", 0)

            def values(layer, c, cols):
                for i, (t0, tn) in enumerate(BLK):
                    free(v.tensor_copy(V[0:tn, i, cols:cols + 512], take((("V", layer, c), i))[0:tn, :]))

            after_empty(dve, ("gate", 1))
            v.scalar_tensor_tensor(out=T_R, in0=Z_R, scalar=-1.0, in1=Z_R, op0=ALU.mult,
                                   op1=ALU.max).then_inc(S("gate_abs"), 1)
            dve.wait_ge(S("gate_ln"), 1)
            step(v.scalar_tensor_tensor(out=Z_R, in0=Z_R, scalar=0.0, in1=L_R, op0=ALU.min, op1=ALU.subtract))
            step(v.tensor_tensor_scan(B_R, C("reset", H4), Z_R, 0.0, ALU.mult, ALU.add))
            step(v.tensor_tensor(SRC_R, I_R, B_R, ALU.subtract))
            step(v.tensor_tensor_scan(T_R, C("minrow", H4), SRC_R, -3e38, ALU.min, ALU.max))
            dve.wait_ge(S("rows_in"), 32)
            seq = lambda row: row[:, TP:NT].rearrange("h (b t) -> h b t", t=TS)
            m0 = mrow[:, :].unsqueeze(2).to_broadcast([H4, NB, TS])
            step(v.tensor_tensor(seq(T_R), seq(T_R), m0, ALU.max))
            step(v.tensor_scalar(NGM_R, T_R, -1.0, None, ALU.mult))
            v.tensor_tensor(MT_R, B_R, T_R, ALU.add)
            wp3 = wprow[:, :].rearrange("h (b t) -> h b t", t=TS)
            v.tensor_tensor(wp3, seq(NGM_R), m0, ALU.add)
            v.tensor_tensor(WE_R[:, 0:TP], SRC_R[:, 0:TP], NGM_R[:, TP - 1:TP].to_broadcast([H4, TP]), ALU.add)
            v.tensor_tensor(seq(WE_R), seq(SRC_R), seq(NGM_R)[:, :, TS - 1:TS].to_broadcast([H4, NB, TS]),
                            ALU.add).then_inc(S("gate_exps_in"), 1)
            after_empty(dve, ("ab", 5, 3))
            after_empty(dve, "carry")
            for k in range(KD):
                cw = lambda j: prow("conv_w", j * KD + k)
                step(v.tensor_scalar(CV[:, k, :], XC[:, k, 0:CW], cw(0), prow("conv_b", k), ALU.mult, ALU.add))
                for j in range(1, NCONV):
                    ins = v.scalar_tensor_tensor(out=CV[:, k, :], in0=XC[:, k, j:j + CW], scalar=cw(j), in1=CV[:, k, :],
                                                 op0=ALU.mult, op1=ALU.add)
                    if j < NCONV - 1:
                        step(ins)
                    else:
                        ins.then_inc(S("conv_sum"), 1)
            values(0, 1, 512)
            for r, X in enumerate((Q, K)):
                after_empty(dve, ("ab", r, 3))
                X4 = X[:, 0:H4, :]
                wide = lambda ap, n: ap.unsqueeze(1).to_broadcast([n, H4, NT])
                sin, cos = C("sin"), C("cos")
                v.tensor_tensor(ROT[64:128], X4[0:64], wide(sin[0:64, :], 64), ALU.mult)
                step(v.tensor_tensor(ROT[0:64], X4[64:128], wide(sin[64:128, :], 64), ALU.mult))
                step(v.tensor_tensor(X4, X4, wide(cos, P), ALU.mult))
                v.tensor_tensor(X4, X4, ROT, ALU.add).then_inc(S("rope_done"), 1)
                dve.wait_ge(S("rope_done"), r + 1)
            values(0, 0, 0)

            def new_states(layer, u, scale):
                slot = ST[:, u % NST]
                for g in range(2):
                    b = take(("ss", layer, u, g))
                    for s in range(4):
                        q = 4 * g + s
                        ins = v.scalar_tensor_tensor(out=slot[:, q, :], in0=slot[:, q, :], scalar=scale(q),
                                                     in1=b[:, s * DH:(s + 1) * DH], op0=ALU.mult, op1=ALU.add)
                    free(ins)

            decay = C("decay").rearrange("p (h n) -> p h n", n=320)
            qdec = C("qdec").rearrange("p (h n) -> p h n", n=SMP)
            mmask = C("mmask")
            for u in range(KD + 1):
                if H4 <= u < KD:
                    b = take(("bc", u))
                    v.tensor_tensor(WB[:, 0:P], b[:, 0:P], mmask[:, 0:P], ALU.add)
                    v.tensor_copy(WB[:, P:TP], b[:, P:TP])
                    v.tensor_tensor(WB[:, TP:384], b[:, P:TP], mmask[:, 0:P], ALU.add)
                    v.tensor_tensor(WB[0:SMP, 384:448], b[0:SMP, TP:NT], mmask[0:SMP, P:192], ALU.add)
                    free(v.tensor_copy(WPS[:, u % 2, :], b[:, NT:NT + SMP]))
                    after_empty(dve, ("bc", u))
                if u > 0:
                    w = u - 1
                    b = take(("num", 0, w))
                    if w < H4:
                        free(v.tensor_copy(OR[:, w, :], b[:, 0:NT]))
                        if w == 0:
                            pass
                    else:
                        free(v.tensor_copy(OR[:, w, :], b[:, 0:NT]))
                        d = take(("den", w))
                        after_empty(dve, ("em", w))
                        step(v.scalar_tensor_tensor(out=rsq[:, :], in0=d[:, 0:NT], scalar=-1.0, in1=EM[:, w % 2, :],
                                                    op0=ALU.mult, op1=ALU.max))
                        free(v.tensor_tensor(rsq[:, :], rsq[:, :], d[:, 0:NT], ALU.max))
                        after_empty(dve, ("den", w))
                        step(v.reciprocal(rsq[:, :], rsq[:, :]))
                        step(v.tensor_tensor(OR[:, w, :], OR[:, w, :], rsq[:, :], ALU.mult))
                        after_empty(dve, ("ab", 7, w - H4))
                        v.tensor_tensor(OR[:, w, :], OR[:, w, :], G[:, w, :], ALU.mult).then_inc(S("o_mlstm"), 1)
                if u < KD:
                    if u == H4:
                        dve.wait_ge(S("keys_scaled"), 1)
                    if u < H4:
                        v.tensor_tensor(QE[:, u % 2, :], Q[:, u, TP:NT], qdec[:, u, :], ALU.mult).then_inc(S("qe0"), 1)
                        b = take(("sc", 0, u))
                        pb = PB[:, u % 2, :]
                        v.tensor_tensor(pb[:, 0:TP], b[:, 0:TP], decay[:, u, 0:TP], ALU.mult)
                        v.tensor_tensor(pb[:, TP:384], b[:, TP:384], decay[:, u, 0:P], ALU.mult)
                        free(v.tensor_tensor(pb[0:SMP, 384:448], b[0:SMP, 384:448], decay[0:SMP, u, TP:320], ALU.mult))
                    else:
                        h = u - H4
                        v.tensor_tensor(QE[:, u % 2, :], Q[:, u, TP:NT], WPS[:, u % 2, :], ALU.mult).then_inc(S("qe0"), 1)
                        dve.wait_ge(S("w_exp"), h + 1)
                        b = take(("sc", 0, u))
                        pb = PB[:, u % 2, :]
                        v.tensor_tensor(pb[:, 0:384], b[:, 0:384], WB[:, 0:384], ALU.mult)
                        free(v.tensor_tensor(pb[0:SMP, 384:448], b[0:SMP, 384:448], WB[0:SMP, 384:448], ALU.mult))
                        n0 = NS0.rearrange("p (b h) -> p b h", h=H4)[:, :, h:h + 1]
                        wps = WPS[:, u % 2, :].rearrange("p (b t) -> p b t", t=TS)
                        qe = QE[:, u % 2, :].rearrange("p (b t) -> p b t", t=TS)
                        no = NOUT[:, 0:32].rearrange("p (b h) -> p b h", h=H4)[:, :, h:h + 1]
                        step(v.tensor_copy(MDEC[:, u % 2, :].unsqueeze(2), wps[:, :, TS - 1:TS]))
                        v.tensor_tensor(no, n0, MDEC[:, u % 2, :].unsqueeze(2), ALU.mult)
                        dve.wait_ge(S("qe0"), u + 1)
                        v.tensor_tensor(wps, qe, n0.to_broadcast([P, NB, TS]), ALU.mult).then_inc(S("qn"), 1)
                if u > 0:
                    w = u - 1
                    if w < H4:
                        new_states(0, w, lambda q: GAMMA[w] ** TS)
                    else:
                        new_states(0, w, lambda q: MDEC[:, w % 2, q:q + 1])
                        after_empty(dve, ("sp", 0, w))
                        h = w - H4
                        no = NOUT[:, 0:32].rearrange("p (b h) -> p b h", h=H4)[:, :, h:h + 1]
                        v.tensor_tensor(no, no, NRAW[:, h, 1:9].unsqueeze(2), ALU.add)
                        ins = v.tensor_copy(NOUT[:, 32 + h:33 + h], NRAW[:, h, 0:1])
                        if w == KD - 1:
                            ins.then_inc(S("n_out"), 1)

            def mix(src, tag, gains, gate):
                for u in range(KD):
                    after_empty(dve, (tag, "var", u))
                    step(v.reciprocal(RS[:, u, :], RS[:, u, :]))
                    ins = v.scalar_tensor_tensor(out=hT[:, u, :], in0=src[:, u, :], scalar=gains(u), in1=RS[:, u, :],
                                                 op0=ALU.mult, op1=ALU.mult)
                    if gate(u):
                        step(ins)
                        ins = v.tensor_tensor(hT[:, u, :], hT[:, u, :], G[:, u, :], ALU.mult)
                    ins.then_inc(S("mix0" if tag == "hn0" else "mix1"), 1)

            mix(OR, "hn0", lambda u: prow("ret_gn", u) if u < H4 else prow("ml_gn", u - H4), lambda u: u < H4)
            for k in range(KD):
                add_to_x(("oab", k), k)
            normed("n1", "ln_ffn", 0)
            for f in range(FT):
                b = take(("fu", f))
                after_empty(dve, ("fg", f))
                free(v.tensor_tensor(FT_A[:, f, :], SG[:, f % 2, :], b[:, 0:NT], ALU.mult))
            for k in range(KD):
                add_to_x(("fd", k), k)

            low = prm[:, PRM["hg_lower"]:PRM["hg_lower"] + 16].rearrange("p (a b) -> p a b", b=8)
            step(v.tensor_tensor(LBT[:, 2, :], low[:, 0, :], low[:, 1, :], ALU.max))
            v.tensor_tensor(LBT[:, 0, :], low[:, 0, :], LBT[:, 2, :], ALU.subtract)
            v.tensor_tensor(LBT[:, 1, :], low[:, 1, :], LBT[:, 2, :], ALU.subtract).then_inc(S("lb_max"), 1)
            dve.wait_ge(S("lb_exp"), 1)
            step(v.tensor_tensor(LBT[:, 2, :], LBT[:, 0, :], LBT[:, 1, :], ALU.add))
            step(v.reciprocal(LBT[:, 2, :], LBT[:, 2, :]))
            step(v.tensor_tensor(LB, LBT[:, 1, :], LBT[:, 2, :], ALU.mult))
            step(v.tensor_scalar(OMLB, LB, -1.0, 1.0, ALU.mult, ALU.add))
            normed("n2", "ln_mix", 8)
            for h in range(HG):
                after_empty(dve, ("c", 2 + h // 4, h % 4))
                v.tensor_scalar(LV[1][:, h, :], K[:, h, :], OMLB[:, h:h + 1], LB[:, h:h + 1], ALU.mult,
                                ALU.add).then_inc(S("forget"), 1)
                dve.wait_ge(S("forget"), h + 1)
                ins = v.tensor_scalar(K[:, h, :], LV[1][:, h, :], -1.0, 1.0, ALU.mult, ALU.add)
                ins.then_inc(S("hgrn_k"), 1)
            values(1, 0, 0)
            values(1, 1, 512)
            for h in range(HG):
                dve.wait_ge(S("forget_ln"), h + 1)
                ins = v.tensor_tensor_scan(CUM[:, h, :], C("reset"), LV[1][:, h, :], 0.0, ALU.mult, ALU.add)
            step(ins)
            after_empty(dve, ("c", 1, 3))

            def level_differences(j):
                L = LV[j % 2]
                ls, lt, _ = halves(L, j)
                cs, ct, ref = halves(CUM, j)
                v.tensor_tensor(lt, ct, ref.to_broadcast(list(ct.shape)), ALU.subtract)
                v.tensor_tensor(ls, ref.to_broadcast(list(cs.shape)), cs, ALU.subtract).then_inc(S("level_diff"), 1)

            def level_queries(j):
                L = LV[j % 2]
                _, lt, _ = halves(L, j)
                _, qt, _ = halves(Q, j)
                dve.wait_ge(S("level_exp"), 8 - j)
                v.tensor_tensor(lt, lt, qt, ALU.mult).then_inc(S("level_q"), 1)

            level = C("level").rearrange("p (j n) -> p j n", n=P)
            diag = lambda h: PH[:, h, 0:512 - 64].rearrange("p n -> p n")

            def level_scores(j):
                if j == 7:
                    for g in range(2):
                        b = take(("lv", j, g))
                        free(v.tensor_copy(PH[:, 4 * g:4 * g + 4, P:TP], b[:, :].rearrange("p (h n) -> p h n", n=P)))
                    return
                for h in range(0, HG, 2):
                    b = take(("lv", j, h))
                    for q in range(2):
                        for i in range(2):
                            at = 0 if i == 0 else TP
                            ins = v.copy_predicated(PH[:, h + q, at:at + P], level[:, j, :].bitcast(mybir.dt.uint32),
                                                    b[:, (2 * q + i) * P:(2 * q + i + 1) * P])
                    free(ins)
                if j < 3:
                    b = take(("lv", j, "s"))
                    mask = level[0:SMP, j, 0:SMP].bitcast(mybir.dt.uint32)
                    for h in range(HG):
                        ins = v.copy_predicated(PH[0:SMP, h, 384:448], mask, b[0:SMP, h * SMP:(h + 1) * SMP])
                    free(ins)

            dve.wait_ge(S("stores"), 16 * 6)
            level_differences(7)
            for h in range(0, HG, 2):
                b = take(("diag", h))
                bv = b[:, :].rearrange("p (h i n) -> p h i n", i=2, n=P)
                for q in range(2):
                    v.tensor_tensor(PH[:, h + q, 0:P], bv[:, q, 0, :], ident, ALU.mult)
                    ins = v.tensor_tensor(PH[:, h + q, TP:384], bv[:, q, 1, :], ident, ALU.mult)
                free(ins)
            b = take(("diag", "s"))
            free(v.tensor_tensor(PH[0:SMP, :, 384:448], b[0:SMP, :].rearrange("p (h n) -> p h n", n=SMP),
                                 ident[0:SMP, 0:SMP].unsqueeze(1).to_broadcast([SMP, HG, SMP]), ALU.mult))
            level_queries(7)
            for j in range(7, -1, -1):
                if j > 0:
                    level_differences(j - 1)
                    level_queries(j - 1)
                level_scores(j)
            end = LV[0]
            v.tensor_tensor(end[:, :, 0:TP], CUM[:, :, TP - 1:TP].to_broadcast([P, HG, TP]), CUM[:, :, 0:TP], ALU.subtract)
            for h in range(HG):
                cs = CUM[:, h, TP:NT].rearrange("p (b t) -> p b t", t=TS)
                ins = v.tensor_tensor(end[:, h, TP:NT].rearrange("p (b t) -> p b t", t=TS),
                                      cs[:, :, TS - 1:TS].to_broadcast([P, NB, TS]), cs, ALU.subtract)
            ins.then_inc(S("end_diff"), 1)
            dve.wait_ge(S("end_exp"), 2)
            v.tensor_tensor(K[:, :, :], K[:, :, :], end[:, :, :], ALU.mult).then_inc(S("hgrn_kend"), 1)
            for h in range(HG):
                v.tensor_tensor(Q[:, h, TP:NT], Q[:, h, TP:NT], ES[:, h, :], ALU.mult).then_inc(S("qe1"), 1)
            for u in range(HG + 1):
                if u > 0:
                    w = u - 1
                    free(v.tensor_copy(OH[:, w, :], take(("num", 1, w))[:, 0:NT]))
                    dec = ES[:, w, :].rearrange("p (b t) -> p b t", t=TS)[:, :, TS - 1]
                    new_states(1, w, lambda q: dec[:, q:q + 1])
            mix(OH, "hn1", lambda u: prow("hg_gn", u), lambda u: True)
            for k in range(KD):
                add_to_x(("oc", k), k)
            normed("n3", "ln_ffn", 8)

            step(v.memset(LG[:, :, :], 0.0))
            b = take("logits")
            v.tensor_copy(LG[:, 0:2, :], b[:, 0:16].rearrange("p (i e) -> p i e", e=NE))
            free(v.tensor_copy(LG[0:SMP, 2, :], b[0:SMP, 16:24]))
            after_empty(dve, "logits")
            c1 = CMP[:, :, :].rearrange("p i (e f) -> p (i e) f", f=NE)
            c2 = CM2[:, :, :].rearrange("p i (e f) -> p (i e) f", f=NE)
            mine = LG[:, :, :].rearrange("p i e -> p (i e)").unsqueeze(2).to_broadcast([P, 3 * NE, NE])
            for i in range(3):
                other = LG[:, i, :].unsqueeze(1).to_broadcast([P, NE, NE])
                me = LG[:, i, :].unsqueeze(2).to_broadcast([P, NE, NE])
                v.tensor_tensor(c1[:, i * NE:(i + 1) * NE, :], other, me, ALU.is_gt)
                v.tensor_tensor(c2[:, i * NE:(i + 1) * NE, :], other, me, ALU.is_equal)
            v.reduce_max(V1[:, :], LG[:, :, :], AX.X)
            step(v.memset(RND[:, :], 0.0))
            step(v.tensor_tensor(CM2[:, :, :], CM2[:, :, :], C("tie").unsqueeze(1).to_broadcast([P, 3, 64]), ALU.mult))
            step(v.tensor_tensor(CMP[:, :, :], CMP[:, :, :], CM2[:, :, :], ALU.add))
            step(v.tensor_reduce(SELM[:, :, :].rearrange("p i e -> p (i e)"), c1, AX.X, ALU.add))
            v.tensor_scalar(SELM[:, :, :], SELM[:, :, :], 1.5, None, ALU.is_lt).then_inc(S("chosen"), 1)
            v.tensor_tensor(GATE[:, :, :], LG[:, :, :], V1[:, :].unsqueeze(2).to_broadcast([P, 3, NE]),
                            ALU.subtract).then_inc(S("router_diff"), 1)
            dve.wait_ge(S("router_exp"), 1)
            dve.wait_ge(S("chosen"), 1)
            step(v.tensor_tensor(GATE[:, :, :], GATE[:, :, :], SELM[:, :, :], ALU.mult))
            step(v.tensor_reduce(V1[:, :], GATE[:, :, :], AX.X, ALU.add))
            step(v.reciprocal(V1[:, :], V1[:, :]))
            step(v.tensor_tensor(GATE[:, :, :], GATE[:, :, :], V1[:, :].unsqueeze(2).to_broadcast([P, 3, NE]), ALU.mult))
            b = take("ranks")
            step(v.memset(RANK[:, :, :], -BIG))
            for i, (t0, tn) in enumerate(BLK):
                step(v.scalar_tensor_tensor(out=RANK[0:tn, i, :], in0=b[0:tn, i * NE:(i + 1) * NE], scalar=BIG,
                                            in1=SELM[0:tn, i, :], op0=ALU.add, op1=ALU.mult))
                step(v.tensor_scalar(RANK[0:tn, i, :], RANK[0:tn, i, :], -BIG, None, ALU.add))
            free(v.reduce_max(RND[:, 0:1], b[:, 24:32], AX.X))
            after_empty(dve, "ranks")
            v.tensor_scalar(RND[:, 1:2], RND[:, 0:1], CAP + 0.5, 8.0, ALU.is_gt, ALU.mult)
            step(v.tensor_scalar(RND[:, 2:3], RND[:, 0:1], 2 * CAP + 0.5, 8.0, ALU.is_gt, ALU.mult))
            step(v.tensor_tensor(RND[:, 3:4], RND[:, 1:2], RND[:, 2:3], ALU.add))
            v.tensor_scalar(NIT[0:1, 0:1], RND[0:1, 3:4], float(NE), None, ALU.add).then_inc(S("rounds_known"), 1)

            def select(dst, e, gated):
                for i, (t0, tn) in enumerate(BLK):
                    rank = RANK[0:tn, i, bass.ds(e, 1)]
                    if gated:
                        ins = v.tensor_scalar(dst[0:tn, i, :], C("slots", tn), rank, GATE[0:tn, i, bass.ds(e, 1)],
                                              ALU.is_equal, ALU.mult)
                    else:
                        ins = v.tensor_scalar(dst[0:tn, i, :], C("slots", tn), rank, None, ALU.is_equal)
                return ins

            def gathered():
                for g in range(2):
                    v.tensor_copy(XG[:, 4 * g:4 * g + 4, :].rearrange("p k n -> p (k n)"),
                                  banks[6 + g][:, :]).then_inc(S("misc_done"), 1)

            select(SE, 0, False).then_inc(S("sel_ready"), 1)
            dve.wait_ge(S("misc_full"), 2)
            gathered()
            dve.wait_ge(S("rounds_known"), 1)
            rounds = dve.value_load(NIT[0:1, 0:1], min_val=NE, max_val=3 * NE)
            with dve.Fori(0, rounds) as it:
                e = it & (NE - 1)
                e1 = (it + 1) & (NE - 1)
                dve.wait_ge(S("misc_done"), it * 10 + 2)
                select(SGE, e, True).then_inc(S("sge_ready"), 1)
                select(SE, e1, False).then_inc(S("sel_ready"), 1)
                for c in range(NFC):
                    dve.wait_ge(S("silu_done"), it * NFC + c + 1)
                    if c >= 2:
                        dve.wait_ge(S("t_full"), it * 12 + c - 1)
                    v.tensor_tensor(AN[:, c % 2, :], SL[:, c % 2, :], banks[c % 2][:, FC:2 * FC],
                                    ALU.mult).then_inc(S("a_ready"), 1)
                dve.wait_ge(S("sge_ready"), it + 1)
                for i in range(3):
                    r = RANK[:, i, bass.ds(e, 1)]
                    v.tensor_scalar(r, r, -float(CAP), None, ALU.add)
                dve.wait_ge(S("misc_full"), it * 10 + 4)
                gathered()
                for m in range(KD):
                    dve.wait_ge(S("misc_full"), it * 10 + m + 5)
                    v.tensor_tensor(xT[:, m, :], xT[:, m, :], banks[6 + m % 2][:, 0:NT],
                                    ALU.add).then_inc(S("misc_done"), 1)
            dve.wait_ge(S("misc_done"), rounds * 10 + 2)
            normed("n4", "ln_final", 0)

        @block.gpsimd
        def _(pool):
            g = nc.gpsimd
            g.memset(XC[:, :, 0:3], 0.0).then_inc(S("history_zero"), 1)

            def src_of(layer, u):
                if layer:
                    return A["state_hgrn"][0, :, u]
                return A["state_ret"][0, :, u] if u < H4 else A["state_mlstm_c"][0, :, u - H4]

            def dst_of(layer, u):
                if layer:
                    return O["hg_s"][0, :, u]
                return O["ret_s"][0, :, u] if u < H4 else O["mc_s"][0, :, u - H4]

            def load_state(layer, u):
                pool.dma_start(ST[:, u % NST], src_of(layer, u).rearrange("b k v -> k b v")).then_inc(
                    S(f"state_in_{layer}_{u % NST}"), 16)

            def store_state(layer, u):
                after_empty(pool, ("ss", layer, u, 1))
                pool.dma_start(dst_of(layer, u).rearrange("b k v -> k b v"), ST[:, u % NST]).then_inc(
                    S(f"state_out_{u % NST}"), 16)

            def spread(layer, u):
                if u >= 1:
                    after_fill(pool, ("ss", layer, u - 1, 1))
                v1 = V[0:SMP, 2, u * DH:(u + 1) * DH].unsqueeze(1).to_broadcast([SMP, NB, DH])
                m = C("bmask", SMP).unsqueeze(2).to_broadcast([SMP, NB, DH])
                g.tensor_tensor(VX[0:SMP], v1, m, ALU.mult).then_inc(S(f"vx{layer}"), 1)

            for u in range(NST):
                load_state(0, u)
            pool.wait_ge(S("conv_sum"), 1)
            pool.wait_ge(S("history_zero"), 1)
            g.tensor_copy(CT[:, :, 0:3], XC[:, :, TP:SX])
            for k in range(KD):
                tail = XC[:, k, SX:XW].rearrange("p (b t) -> p b t", t=3 + TS)[:, :, TS:TS + 3]
                ins = g.tensor_copy(CT[:, k, 3:27].rearrange("p (b t) -> p b t", t=3), tail)
            ins.then_inc(S("conv_tail"), 1)
            pool.wait_ge(S("conv_silu"), KD)
            g.tensor_scalar(K[:, H4:KD, :], K[:, H4:KD, :], DH ** -0.5, None, ALU.mult).then_inc(S("keys_scaled"), 1)
            after_empty(pool, (("V", 0, 0), 2))
            stored = [0] * NST
            for layer in range(2):
                if layer:
                    after_empty(pool, (("V", 1, 1), 2))
                    for u in range(NST):
                        pool.wait_ge(S(f"state_out_{u}"), 16 * stored[u])
                        load_state(1, u)
                    for j in range(7, -1, -1):
                        pool.wait_ge(S("level_exp"), 8 - j)
                        ls, ks = halves(LV[j % 2], j)[0], halves(K, j)[0]
                        g.tensor_tensor(ls, ls, ks, ALU.mult).then_inc(S("level_k"), 1)
                for u in range(KD + 1):
                    if u < KD:
                        spread(layer, u)
                    if u > 0:
                        store_state(layer, u - 1)
                        stored[(u - 1) % NST] += 1
                        if u - 1 + NST < KD:
                            pool.wait_ge(S(f"state_out_{(u - 1) % NST}"), 16 * stored[(u - 1) % NST])
                            load_state(layer, u - 1 + NST)
            for s in range(NST):
                pool.wait_ge(S(f"state_out_{s}"), 16 * stored[s])


_IN = ["x_prompt", "x_sample", "state_ret", "state_mlstm_c", "state_mlstm_n", "state_mlstm_m", "state_conv",
       "state_hgrn", "ln_mix", "ln_ffn", "ln_final", "w_in_ab", "b_gates_ab", "conv_w_ab", "conv_b_ab", "ret_gn",
       "ml_gn", "w_out_ab", "w_in_c", "hg_lower", "hg_gn", "w_out_c", "w_ffn_gate", "w_ffn_up", "w_ffn_down",
       "w_router", "b_router", "w_moe_gate", "w_moe_up", "w_moe_down"]
_OUT = [("y_prompt", (1, TP, D)), ("y_sample", (NB, TS, D)),
        ("ret_p", (1, 1, 4, DH, DH)), ("ret_s", (1, NB, 4, DH, DH)),
        ("mc_p", (1, 1, 4, DH, DH)), ("mc_s", (1, NB, 4, DH, DH)),
        ("mn_p", (1, 1, 4, DH)), ("mn_s", (1, NB, 4, DH)),
        ("mm_p", (1, 1, 4)), ("mm_s", (1, NB, 4)),
        ("conv_p", (1, 1, 3, D)), ("conv_s", (1, NB, 3, D)),
        ("hg_p", (1, 1, HG, DH, DH)), ("hg_s", (1, NB, HG, DH, DH))]


def kernel(**inputs):
    import concourse.bacc as bacc
    from concourse.bass_utils import run_bass_kernel_spmd

    nc = bacc.Bacc("TRN2", target_bir_lowering=False, num_devices=1)
    arrays = {f"in_{name}": np.ascontiguousarray(inputs[name]) for name in _IN}
    arrays["in_cst"] = constants()
    ins = {name[3:]: nc.dram_tensor(name, a.shape, F32, kind="ExternalInput").ap() for name, a in arrays.items()}
    outs = {name: nc.dram_tensor(f"out_{name}", shape, F32, kind="ExternalOutput").ap() for name, shape in _OUT}
    trunk_kernel(nc, ins, outs)
    r = run_bass_kernel_spmd(nc, [arrays], core_ids=[0])
    return tuple(r.results[0][f"out_{name}"] for name, _ in _OUT)
```

```python
import math
from contextlib import ExitStack

import numpy as np

import concourse.bass as bass
from concourse import mybir

F32 = mybir.dt.float32
I32 = mybir.dt.int32
F32R = mybir.dt.float32r
ALU = mybir.AluOpType
ACT = mybir.ActivationFunctionType
AX = mybir.AxisListType

P = 128
D = 1024
KD = D // P
TP = 256
NB, TS = 8, 8
SMP = NB * TS
NT = TP + SMP
BLK = [(0, 128), (128, 128), (256, 64)]
H4 = 4
HG = 8
DH = 128
FF = 2816
FT = FF // P
NE = 8
PAST = 2048
EPS = 1e-6
NCONV = 4
XW = 3 + TP + NB * (3 + TS)
CW = XW - 3
SX = 3 + TP
FC = 256
NFC = FF // FC
UNIT = 2048
DSTAGE = 2
DSPLIT = 2
NST = 3
NSTAGE = 7
NSPLIT = 3
CAP = 128
BIG = 1024.0
GAMMA = [1.0 - 2.0 ** (-5.0 - h) for h in range(H4)]

CONST = {}
_at = 0
for _name, _width in (("ident", P), ("ones", P), ("inv_d", P), ("eps", 1), ("pick", 16), ("center", P),
                      ("cos", NT), ("sin", NT), ("decay", H4 * 320), ("qdec", H4 * SMP), ("kdec", 3 * H4),
                      ("mmask", 192), ("reset", NT), ("minrow", NT), ("level", 7 * P), 
                      ("bmask", NB), ("slots", CAP), ("tri", P), ("tie", 64)):
    CONST[_name] = (_at, _width)
    _at += _width
NCONST = _at
NFIRST = CONST["pick"][0]

PRM = {}
_at = 0
for _name, _rows in (("ln_mix", 16), ("ln_ffn", 16), ("ln_final", 8), ("conv_w", 32), ("conv_b", 8),
                     ("ret_gn", 4), ("ml_gn", 4), ("hg_lower", 16), ("hg_gn", 8)):
    PRM[_name] = _at
    _at += _rows
NPRM = _at


def constants():
    c = np.zeros((P, NCONST), np.float32)

    def put(name, value):
        a, w = CONST[name]
        value = np.asarray(value, np.float64).reshape(len(value), w)
        c[:len(value), a:a + w] = value.astype(np.float32)

    p = np.arange(P)
    put("ident", np.eye(P))
    put("ones", np.ones((P, P)))
    put("inv_d", np.full((P, P), 1.0 / D))
    pick = np.zeros((P, 16))
    pick[:, KD - 1] = 1.0 / DH
    put("pick", pick)
    put("center", np.eye(P) - 1.0 / DH)
    half = DH // 2
    inv = (10000.0 ** (-(np.arange(half, dtype=np.float32) / np.float32(half)).astype(np.float64))).astype(np.float32)
    pos = np.concatenate([np.arange(TP), PAST + np.tile(np.arange(TS), NB)]).astype(np.float32)
    ang = (pos[None, :] * inv[:, None]).astype(np.float32).astype(np.float64)
    put("cos", np.concatenate([np.cos(ang), np.cos(ang)]))
    put("sin", np.concatenate([np.sin(ang), -np.sin(ang)]))
    scale = DH ** -0.5
    s, t = p[:, None], np.arange(TP)[None, :]
    s8, t8 = np.arange(SMP)[:, None], np.arange(SMP)[None, :]
    same = (s8 // TS == t8 // TS) & (t8 >= s8)
    decay = np.zeros((P, H4, 320))
    qdec = np.zeros((P, H4, SMP))
    kdec = np.zeros((P, 3, H4))
    for h, g in enumerate(GAMMA):
        decay[:, h, :TP] = np.where(t >= s, g ** np.maximum(t - s, 0), 0) * scale
        decay[:SMP, h, TP:] = np.where(same, g ** np.maximum(t8 - s8, 0), 0) * scale
        qdec[:, h, :] = (g ** (np.arange(SMP) % TS + 1.0))[None, :] * scale
        kdec[:, 0, h] = g ** (TP - 1.0 - p)
        kdec[:, 1, h] = g ** (TP - 1.0 - P - p)
        kdec[:SMP, 2, h] = g ** (TS - 1.0 - np.arange(SMP) % TS)
    put("decay", decay)
    put("qdec", qdec)
    put("kdec", kdec)
    mmask = np.zeros((P, 192))
    mmask[:, :P] = np.where(p[None, :] >= s, 0, -1e30)
    mmask[:SMP, P:] = np.where(same, 0, -1e30)
    put("mmask", mmask)
    start = np.zeros(NT, bool)
    start[0] = True
    start[TP::TS] = True
    put("reset", np.tile(np.where(start, 0.0, 1.0), (P, 1)))
    put("minrow", np.tile(np.where(start, -3e38, 3e38), (P, 1)))
    level = np.zeros((P, 7, P))
    for j in range(7):
        m = 1 << j
        level[:, j, :] = (s // (2 * m) == p[None, :] // (2 * m)) & (s % (2 * m) < m) & (p[None, :] % (2 * m) >= m)
    put("level", level)
    put("bmask", (np.arange(SMP)[:, None] // TS == np.arange(NB)[None, :]))
    put("slots", np.tile(np.arange(CAP), (P, 1)))
    put("tri", s < p[None, :])
    e = np.arange(NE)
    put("tie", np.tile((e[None, :] < e[:, None]).reshape(1, 64), (P, 1)))
    put("eps", np.full((P, 1), EPS))
    return c


def trunk_kernel(nc, A, O):
    with ExitStack() as ctx:
        def sb(name, shape, dt=F32):
            return ctx.enter_context(nc.sbuf_tensor(name, shape, dt))

        sems = {}

        def S(name):
            if name not in sems:
                sems[name] = ctx.enter_context(nc.semaphore(name))
            return sems[name]

        banks = [ctx.enter_context(nc.psum_tensor(f"bank{i}", [P, 512], F32)) for i in range(8)]

        base = -(-nc.sbuf_base // 32) * 32
        RING = (DSTAGE + 2 * DSPLIT) * UNIT
        ring = sb("ring", [P, RING])
        hT = sb("hT", [P, KD, NT])
        arena = sb("arena", [P, 26880])
        AT_RING, AT_HT, AT_ARENA = 0, RING, RING + KD * NT

        def parts(name, at, *shape):
            assert at % 8 == 0
            return nc.alloc_sbuf_tensor_at(name, [P, *shape], F32R, offset=base + 4 * at)

        cst = sb("cst", [P, NCONST])
        xT = sb("xT", [P, KD, NT])
        prm = sb("prm", [P, NPRM])
        wgate = sb("wgate", [P, KD, 2 * H4])
        wrt = sb("wrt", [P, KD, NE])
        brt = sb("brt", [NE, 1])
        gbias = sb("gbias", [H4, 2])
        mrow = sb("mrow", [H4, NB])
        small = sb("small", [P, 512])

        def C(name, rows=P):
            a, w = CONST[name]
            return cst[0:rows, a:a + w]

        def prow(name, k):
            return prm[:, PRM[name] + k:PRM[name] + k + 1]

        ident = C("ident")

        def spread_row(rows, u):
            return ident[0:rows, u:u + 1].to_broadcast([rows, P])

        ones = C("ones")

        def region(at, *shape):
            n = math.prod(shape)
            v = arena[:, at:at + n]
            if len(shape) == 1:
                return v
            if len(shape) == 2:
                return v.rearrange("p (a b) -> p a b", b=shape[1])
            return v.rearrange("p (a b c) -> p a b c", b=shape[1], c=shape[2])

        Q = region(0, KD, NT)
        K = region(2560, KD, NT)
        G = region(5120, KD, NT)
        V = region(7680, 3, D)
        ST = region(10752, NST, NB, DH)
        KN = region(13824, 2, 3, DH)
        VX = region(14592, NB, DH)
        XC = region(15616, KD, XW)
        CV = region(18392, KD, CW)
        PB = region(21168, 2, 448)
        OR = region(22064, KD, NT)
        WB = region(24624, 448)
        EM = region(25072, 2, NT)
        ROW = region(25712, 3, NT)
        SQH = region(15616, KD, NT)
        ROT = region(13824, H4, NT)
        CUM = region(15616, KD, NT)
        LV = [region(18176, KD, NT), region(20736, KD, NT)]
        PH = region(23296, HG, 448)
        OH = region(20736, KD, NT)
        XN = region(0, 3, D)
        PN = region(3072, P)
        CN = region(3200, D)
        NN = region(4224, P)
        CT = region(24624, KD, 27)
        CO = arena[0:27, 19152:19152 + D]
        FTH, FTL = parts("ff_hi", AT_ARENA, FT, NT), parts("ff_lo", AT_ARENA + FT * NT, FT, NT)
        NSG = 4
        SG = region(14080, NSG, NT)
        SQF = {"n0": region(7680, KD, NT), "n1": region(15360, KD, NT), "n2": region(15360, KD, NT),
               "n3": region(7680, KD, NT), "n4": region(20736, KD, NT)}
        HH = parts("h_hi", AT_HT, KD, NT)
        NX2 = region(10752, KD, NT)
        HL_A, HL_C, HL_O = parts("h_lo_a", AT_ARENA + 22064, KD, NT), parts("h_lo_c", AT_ARENA + 10752, KD, NT), \
            parts("h_lo_o", AT_ARENA + 20736, KD, NT)
        HN = ring[:, 9216:9216 + 3 * D].rearrange("p (i d) -> p i d", d=D)
        HNH, HNL = parts("hn_hi", AT_ARENA, 3, D), parts("hn_lo", AT_ARENA + 3072, 3, D)
        SE = parts("selection", AT_ARENA + 6144, 3, CAP)
        SGE = region(6528, 3, CAP)
        STH = parts("spread", AT_ARENA + 6912, NT)
        YH, YL = parts("y_hi", AT_ARENA + 8192, D), parts("y_lo", AT_ARENA + 9216, D)
        ATH, ATL = parts("at_hi", AT_ARENA + 10240, 2, FC), parts("at_lo", AT_ARENA + 10752, 2, FC)
        AN = region(11264, 2, FC)
        SL = region(11776, 2, FC)
        XGH, XGL = parts("xg_hi", AT_HT, KD, CAP), parts("xg_lo", AT_HT + 1024, KD, CAP)
        STAGE = region(12544, NSTAGE, UNIT)
        WH = [parts(f"w_hi_{i}", AT_RING + 2 * UNIT * i, UNIT) for i in range(NSPLIT)]
        WL = [parts(f"w_lo_{i}", AT_RING + 2 * UNIT * i + UNIT, UNIT) for i in range(NSPLIT)]
        YN = region(15616, 3, D)
        UNITS = []
        for c in range(NFC):
            UNITS += [("a", c), ("b", c)] + ([("d", c - 2)] if c >= 2 else [])
        UNITS += [("d", NFC - 2), ("d", NFC - 1)]
        NU = len(UNITS)
        assert NU % NSPLIT == 0
        turn_of = {u: p for p, u in enumerate(UNITS)}
        stage_uses = [len(range(i, NU, NSTAGE)) for i in range(NSTAGE)]

        SRC = small[:, 0:24].rearrange("p (c r h) -> p c r h", c=3, r=2)
        NS0 = small[:, 24:56]
        NRAW = small[:, 56:92].rearrange("p (h n) -> p h n", n=9)
        NOUT = small[:, 92:128]
        LB = small[:, 128:136]
        OMLB = small[:, 136:144]
        LBT = small[:, 144:168].rearrange("p (a b) -> p a b", b=8)
        QE = small[:, 168:296].rearrange("p (a b) -> p a b", b=SMP)
        WPS = small[:, 296:424].rearrange("p (a b) -> p a b", b=SMP)
        rows = sb("rows", [H4, 6, NT])
        I_R, B_R, SRC_R, NGM_R, MT_R, WE_R = [rows[:, i, :] for i in range(6)]
        Z_R, L_R, T_R = [ROW[0:H4, i, :] for i in range(3)]
        wprow = sb("wprow", [H4, SMP])
        SPO = sb("SPO", [P, 2, DH])
        ES = C("decay")[:, 0:HG * SMP].rearrange("p (h n) -> p h n", n=SMP)
        NTO = region(24624 + 0, P)[0:36]
        LGT = region(6528, NT)[0:NE]
        LG = region(7232, 3, NE)
        CMP = region(7256, 3, 64)
        CM2 = region(7448, 3, 64)
        SELM = region(7640, 3, NE)
        GATE = region(7664, 3, NE)
        RANK = region(7688, 3, NE)
        V1 = sb("V1", [P, 3])
        WGH, WGL = sb("wgate_hi", [P, KD, 2 * H4], F32R), sb("wgate_lo", [P, KD, 2 * H4], F32R)
        GS = sb("GS", [P, 1])
        RND = sb("RND", [P, 4])
        NIT = sb("NIT", [1, 1], I32)
        rsq = sb("rsq", [P, NT])
        MDEC = sb("MDEC", [P, 2, NB])

        DST = [ring[:, i * UNIT:(i + 1) * UNIT] for i in range(DSTAGE)]
        DWH = [parts(f"dense_hi_{i}", AT_RING + (DSTAGE + 2 * i) * UNIT, UNIT) for i in range(DSPLIT)]
        DWL = [parts(f"dense_lo_{i}", AT_RING + (DSTAGE + 2 * i + 1) * UNIT, UNIT) for i in range(DSPLIT)]

        w_ab = A["w_in_ab"][0].rearrange("(k p) n -> p k n", p=P)
        w_oab = A["w_out_ab"][0].rearrange("(k p) n -> p k n", p=P)
        w_c = A["w_in_c"][0].rearrange("(k p) n -> p k n", p=P)
        w_oc = A["w_out_c"][0].rearrange("(k p) n -> p k n", p=P)
        w_fg = A["w_ffn_gate"][0].rearrange("(k p) n -> p k n", p=P)
        w_fu = A["w_ffn_up"][0].rearrange("(k p) n -> p k n", p=P)
        w_fd = A["w_ffn_down"][0].rearrange("(k p) n -> p k n", p=P)
        AB_ORDER = [4, 5, 6, 0, 1, 2, 3, 7]
        C_ORDER = [2, 3, 0, 1, 4, 5, 6, 7]
        plan = [(kind, c, half) for kind, order in (("ab", AB_ORDER), ("oab", range(2)), ("ffn", range(NFC)),
                                                    ("fd", range(KD)), ("c", C_ORDER), ("oc", range(2)))
                for c in order for half in range(2)]
        NDENSE = len(plan)
        place = {key: n for n, key in enumerate(plan)}
        dense_landed = [S(f"dense_landed_{s}") for s in range(DSTAGE)]
        stage_landed = [S(f"stage_landed_{s}") for s in range(NSTAGE)]

        def unit_view(n, buffers):
            kind = plan[n][0]
            w = buffers[n % len(buffers)]
            if kind == "fd":
                return w[:, 0:FT // 2 * P].rearrange("p (k n) -> p k n", n=P)
            return w[:, 0:UNIT].rearrange("p (k n) -> p k n", n=256)

        def unit_flat(n, buffers):
            return buffers[n % len(buffers)][:, 0:FT // 2 * P if plan[n][0] == "fd" else UNIT]

        filled = {"act": S("filled_for_act"), "dve": S("filled_for_dve")}
        emptied = {"act": S("emptied_by_act"), "dve": S("emptied_by_dve")}
        count = {"act": 0, "dve": 0}
        ticket = {}
        unit_read = {}

        def bank_of(kind, n):
            return banks[(0 if kind == "act" else 4) + n % 4]

        def after_fill(eng, name):
            kind, n = ticket[name]
            eng.wait_ge(filled[kind], n + 1)

        def after_empty(eng, name):
            kind, n = ticket[name]
            eng.wait_ge(emptied[kind], n + 1)

        def halves(X, j):
            m = 1 << j
            if j >= 3:
                w = X[:, :, 0:TP]
                if j == 7:
                    return w[:, :, 0:P], w[:, :, P:TP], w[:, :, P - 1:P]
                w = w.rearrange("p h (n m) -> p h n m", m=2 * m)
                return w[:, :, :, 0:m], w[:, :, :, m:2 * m], w[:, :, :, m - 1:m]
            w = X.rearrange("p h (n m) -> p (h n) m", m=2 * m)
            return w[:, :, 0:m], w[:, :, m:2 * m], w[:, :, m - 1:m]

        block = ctx.enter_context(nc.Block())

        @block.tensor
        def _(pe):
            mm = nc.tensor.matmul

            def open_bank(kind):
                n = count[kind]
                if n >= 4:
                    pe.wait_ge(emptied[kind], n - 3)
                return bank_of(kind, n)

            def close_bank(kind, ins, name):
                assert name not in ticket
                ticket[name] = (kind, count[kind])
                count[kind] += 1
                ins.then_inc(filled[kind], 1)

            def need_unit(*key):
                n = place[key]
                pe.wait_ge(S("dense_split"), n + 1)
                return unit_view(n, DWH), unit_view(n, DWL)

            def used_unit(key, kind, name):
                unit_read[place[key]] = (filled[kind], ticket[name][1] + 1)

            def product3(out, left, right, start, stop):
                mm(out, left[0], right[0], start=start, stop=False)
                mm(out, left[0], right[1], start=False, stop=False)
                return mm(out, left[1], right[0], start=False, stop=stop)

            def gemm_tile(w, cols, src, kind, name, ks, ready=None):
                b = open_bank(kind)
                for k in range(ks):
                    if ready is not None:
                        pe.wait_ge(S(ready), k + 1)
                    ins = product3(b[:, 0:NT], [x[:, k, cols:cols + P] for x in w], [x[:, k, :] for x in src],
                                   k == 0, k == ks - 1)
                close_bank(kind, ins, name)

            def token_tiles(w, src, key, tag):
                for i, (t0, tn) in enumerate(BLK):
                    b = open_bank("dve")
                    for k in range(KD):
                        ins = product3(b[0:tn, 0:256], [x[:, k, t0:t0 + tn] for x in src], [x[:, k, :] for x in w],
                                       k == 0, k == KD - 1)
                    close_bank("dve", ins, (tag, key[2], i))
                used_unit(key, "dve", (tag, key[2], 2))

            def rms(tag):
                b = open_bank("act")
                for k in range(KD):
                    pe.wait_ge(S(tag + "_squares"), k + 1)
                    ins = mm(b[:, 0:NT], C("inv_d"), SQF[tag][:, k, :], start=(k == 0), stop=(k == KD - 1))
                close_bank("act", ins, (tag, "ms"))

            def center(u):
                if u < H4:
                    after_empty(pe, ("num", 0, u))
                else:
                    pe.wait_ge(S("o_mlstm"), u - H4 + 1)
                b = open_bank("act")
                ins = mm(b[:, 0:NT], C("center"), OR[:, u, :], start=True, stop=True)
                close_bank("act", ins, ("cen", u))

            def head_scales(tag):
                b = open_bank("act")
                for u in range(KD):
                    if tag == "hn0":
                        after_empty(pe, ("cen", u))
                    else:
                        pe.wait_ge(S("hn1_squares"), u + 1)
                    ins = mm(b[0:KD, 0:NT], C("pick")[:, KD - 1 - u:2 * KD - 1 - u], SQH[:, u, :],
                             start=(u == 0), stop=(u == KD - 1))
                close_bank("act", ins, (tag, "var"))
                pe.wait_ge(S(tag + "_scales"), 1)
                for u in range(KD):
                    b = open_bank("dve")
                    ins = mm(b[:, 0:NT], spread_row(KD, u), rsq[0:KD, :], start=True, stop=True)
                    close_bank("dve", ins, (tag, "scale", u))

            pe.wait_ge(S("const_in"), 16)
            pe.wait_ge(S("x_in"), 32)
            for k in range(KD):
                b = open_bank("dve")
                for i, (t0, tn) in enumerate(BLK):
                    ins = nc.tensor.transpose(b[:, t0:t0 + tn], XN[0:tn, i, k * P:(k + 1) * P], ident[0:tn, 0:tn])
                close_bank("dve", ins, ("xT", k))
            rms("n0")
            pe.wait_ge(S("prm_in"), 16 * 9)
            b = open_bank("act")
            ins = nc.tensor.transpose(b[:, 0:NPRM], PN[0:NPRM, :], ident[0:NPRM, 0:NPRM])
            close_bank("act", ins, "prm")
            pe.wait_ge(S("carry_in"), 32)
            b = open_bank("act")
            for k in range(KD):
                nc.tensor.transpose(b[:, 24 * k:24 * k + 24], CN[0:24, k * P:(k + 1) * P], ident[0:24, 0:24])
            ins = nc.tensor.transpose(b[:, 192:224], NN[0:32, :], ident[0:32, 0:32])
            close_bank("act", ins, "carry")

            HA = (HH, HL_A)
            for c in AB_ORDER:
                for half in range(2):
                    key = ("ab", c, half)
                    w = need_unit(*key)
                    if c in (2, 6):
                        token_tiles(w, HA, key, ("V", 0, c // 6))
                        continue
                    for j in range(2):
                        first = c == AB_ORDER[0] and half == 0 and j == 0
                        gemm_tile(w, j * P, HA, "act", ("ab", c, 2 * half + j), KD, "n0_h" if first else None)
                    used_unit(key, "act", ("ab", c, 2 * half + 1))
                if c == 5:
                    pe.wait_ge(S("wgate_split"), 1)
                    for r in range(2):
                        b = open_bank("act")
                        for k in range(KD):
                            ins = product3(b[0:H4, 0:NT], [x[:, k, r * H4:(r + 1) * H4] for x in (WGH, WGL)],
                                           [x[:, k, :] for x in HA], k == 0, k == KD - 1)
                        close_bank("act", ins, ("gate", r))
            pe.wait_ge(S("gate_exps"), 2)
            b = open_bank("act")
            for i, (t0, tn) in enumerate(BLK):
                for r, row in enumerate((SRC_R, WE_R)):
                    ins = nc.tensor.transpose(b[0:tn, 8 * i + 4 * r:8 * i + 4 * r + 4], row[:, t0:t0 + tn],
                                              ident[0:H4, 0:H4])
            close_bank("act", ins, "cols")
            pe.wait_ge(S("conv_tail"), 1)
            for g in range(2):
                b = open_bank("act")
                for k in range(4):
                    ins = nc.tensor.transpose(b[0:27, k * P:(k + 1) * P], CT[:, 4 * g + k, :], ident)
                close_bank("act", ins, ("conv_out", g))

            def scores(u):
                b = open_bank("dve")
                mm(b[:, 0:TP], K[:, u, 0:P], Q[:, u, 0:TP], start=True, stop=True)
                mm(b[:, TP:TP + P], K[:, u, P:TP], Q[:, u, P:TP], start=True, stop=True)
                ins = mm(b[0:SMP, 384:448], K[:, u, TP:NT], Q[:, u, TP:NT], start=True, stop=True)
                close_bank("dve", ins, ("sc", 0, u))

            def turn_keys(layer, u):
                b = open_bank("act")
                for i, (t0, tn) in enumerate(BLK):
                    ins = nc.tensor.transpose(b[0:tn, i * P:(i + 1) * P], K[:, u, t0:t0 + tn], ident)
                close_bank("act", ins, ("kn", layer, u))

            def weigh(b, left, probs, right, states):
                mm(b[:, 0:TP], left(0), probs[:, 0:TP], start=True, stop=False, skip_group_check=True)
                mm(b[:, P:TP], left(1), probs[:, TP:TP + P], start=False, stop=False, skip_group_check=True)
                ins = mm(b[:, TP:NT], left(2), probs[0:SMP, 384:448], start=False, stop=False, skip_group_check=True)
                if states is None:
                    return mm(b[:, TP:NT], ones, right, start=False, stop=True, skip_group_check=True)
                for s in range(NB):
                    ins = mm(b[:, TP + s * TS:TP + (s + 1) * TS], states[:, s, :], right[:, s * TS:(s + 1) * TS],
                             start=False, stop=(s == NB - 1), skip_group_check=True)
                return ins

            def outputs(layer, u, probs, probs_ready, right):
                values = lambda i: V[0:BLK[i][1], i, u * DH:(u + 1) * DH]
                probs_ready()
                pe.wait_ge(S(f"qe{layer}"), u + 1)
                pe.wait_ge(S(f"state_in_{layer}_{u % NST}"), 16 * (u // NST + 1))
                b = open_bank("dve")
                ins = weigh(b, values, probs, right, ST[:, u % NST])
                close_bank("dve", ins, ("num", layer, u))
                if layer == 0 and u >= H4:
                    b = open_bank("dve")
                    pe.wait_ge(S("qn"), u - H4 + 1)
                    ins = weigh(b, lambda i: ones[0:BLK[i][1], :], probs, WPS[:, u % 2, :], None)
                    close_bank("dve", ins, ("den", u))

            def state(layer, u):
                after_empty(pe, ("kn", layer, u))
                kn = KN[:, u % 2]
                v = lambda i: V[0:BLK[i][1], i, u * DH:(u + 1) * DH]
                b = open_bank("act")
                mm(b[:, 0:DH], kn[:, 0, :], v(0), start=True, stop=False)
                ins = mm(b[:, 0:DH], kn[:, 1, :], v(1), start=False, stop=True)
                if layer == 0 and u >= H4:
                    mm(b[:, DH:DH + 1], kn[:, 0, :], ones[:, 0:1], start=True, stop=False)
                    mm(b[:, DH:DH + 1], kn[:, 1, :], ones[:, 0:1], start=False, stop=True)
                    ins = mm(b[:, DH + 1:DH + 9], kn[0:SMP, 2, :], C("bmask", SMP), start=True, stop=True)
                close_bank("act", ins, ("sp", layer, u))
                pe.wait_ge(S(f"vx{layer}"), u + 1)
                for g in range(2):
                    b = open_bank("dve")
                    ins = mm(b[:, :].rearrange("p (b v) -> p b v", v=DH), kn[0:SMP, 2, :],
                             VX[0:SMP, 4 * g:4 * g + 4, :], start=True, stop=True)
                    close_bank("dve", ins, ("ss", layer, u, g))

            pe.wait_ge(S("rope_done"), 2)
            for u in range(KD + 1):
                if H4 <= u < KD:
                    h = u - H4
                    sel = spread_row(H4, h)
                    b = open_bank("dve")
                    mm(b[:, 0:NT], sel, NGM_R, start=True, stop=True)
                    ins = mm(b[:, NT:NT + SMP], sel, wprow[:, :], start=True, stop=True)
                    close_bank("dve", ins, ("bc", u))
                    b = open_bank("act")
                    ins = mm(b[:, 0:NT], sel, MT_R, start=True, stop=True)
                    close_bank("act", ins, ("em", u))
                if u > 0:
                    outputs(0, u - 1, PB[:, (u - 1) % 2, :], lambda: after_empty(pe, ("sc", 0, u - 1)), QE[:, (u - 1) % 2, :])
                if u < KD:
                    if u == H4:
                        pe.wait_ge(S("keys_scaled"), 1)
                    scores(u)
                    turn_keys(0, u)
                if u > 0:
                    state(0, u - 1)
                if u > 1:
                    center(u - 2)
            pe.wait_ge(S("n_out"), 1)
            b = open_bank("act")
            ins = nc.tensor.transpose(b[0:36, 0:P], NOUT, ident)
            close_bank("act", ins, "n_out")
            center(KD - 1)
            head_scales("hn0")

            def projection_out(kind, src):
                for c in range(2):
                    for half in range(2):
                        w = need_unit(kind, c, half)
                        for j in range(2):
                            k = 4 * c + 2 * half + j
                            gemm_tile(w, j * P, src, "dve", (kind, k), KD,
                                      {"oab": "mix0_h", "oc": "mix1_h"}[kind] if k == 0 else None)
                        used_unit((kind, c, half), "dve", (kind, k))

            projection_out("oab", HA)

            rms("n1")
            for f in range(FT):
                key = ("ffn", f // 2, f % 2)
                w = need_unit(*key)
                gemm_tile(w, 0, HA, "act", ("fg", f), KD, "n1_h" if f == 0 else None)
                gemm_tile(w, P, HA, "dve", ("fu", f), KD)
                used_unit(key, "dve", ("fu", f))
            for m in range(KD):
                b = open_bank("dve")
                for half in range(2):
                    w = need_unit("fd", m, half)
                    for q in range(FT // 2):
                        k = FT // 2 * half + q
                        if m == 0:
                            pe.wait_ge(S("ff_ready"), k + 1)
                        ins = product3(b[:, 0:NT], [x[:, q, :] for x in w], [x[:, k, :] for x in (FTH, FTL)],
                                       k == 0, k == FT - 1)
                    if half == 0:
                        ins.then_inc(S("fd_half_used"), 1)
                        unit_read[place[("fd", m, 0)]] = (S("fd_half_used"), m + 1)
                close_bank("dve", ins, ("fd", m))
                used_unit(("fd", m, 1), "dve", ("fd", m))

            rms("n2")
            HC = (HH, HL_C)
            def same_scores():
                pe.wait_ge(S("hgrn_k"), HG)
                after_empty(pe, ("c", 1, 3))
                for h in range(0, HG, 2):
                    b = open_bank("dve")
                    for j in range(2):
                        for i in range(2):
                            at = slice(i * P, (i + 1) * P)
                            ins = mm(b[:, (2 * j + i) * P:(2 * j + i + 1) * P], K[:, h + j, at], Q[:, h + j, at],
                                     start=True, stop=True)
                    close_bank("dve", ins, ("diag", h))
                b = open_bank("dve")
                for h in range(HG):
                    ins = mm(b[0:SMP, h * SMP:(h + 1) * SMP], K[:, h, TP:NT], Q[:, h, TP:NT], start=True, stop=True)
                close_bank("dve", ins, ("diag", "s"))

            def level_scores(j):
                L = LV[j % 2]
                pe.wait_ge(S("level_k"), 8 - j)
                pe.wait_ge(S("level_q"), 8 - j)
                if j == 7:
                    for g in range(2):
                        b = open_bank("dve")
                        for h in range(4):
                            ins = mm(b[:, h * P:(h + 1) * P], L[:, 4 * g + h, 0:P], L[:, 4 * g + h, P:TP],
                                     start=True, stop=True)
                        close_bank("dve", ins, ("lv", j, g))
                    return
                for h in range(0, HG, 2):
                    b = open_bank("dve")
                    for q in range(2):
                        for i in range(2):
                            at = slice(i * P, (i + 1) * P)
                            ins = mm(b[:, (2 * q + i) * P:(2 * q + i + 1) * P], L[:, h + q, at], L[:, h + q, at],
                                     start=True, stop=True)
                    close_bank("dve", ins, ("lv", j, h))
                if j < 3:
                    b = open_bank("dve")
                    for h in range(HG):
                        ins = mm(b[0:SMP, h * SMP:(h + 1) * SMP], L[:, h, TP:NT], L[:, h, TP:NT], start=True, stop=True)
                    close_bank("dve", ins, ("lv", j, "s"))

            for c in C_ORDER:
                for half in range(2):
                    key = ("c", c, half)
                    w = need_unit(*key)
                    if c in (4, 5):
                        token_tiles(w, HC, key, ("V", 1, c - 4))
                    else:
                        for j in range(2):
                            first = c == C_ORDER[0] and half == 0 and j == 0
                            gemm_tile(w, j * P, HC, "act", ("c", c, 2 * half + j), KD, "n2_h" if first else None)
                        used_unit(key, "act", ("c", c, 2 * half + 1))
                    if c >= 4:
                        i = 2 * (c - 4) + half
                        if i == 0:
                            same_scores()
                        else:
                            level_scores(8 - i)
            level_scores(0)
            for u in range(HG + 1):
                if u > 0:
                    outputs(1, u - 1, PH[:, u - 1, :], lambda: None, Q[:, u - 1, TP:NT])
                if u < HG:
                    pe.wait_ge(S("hgrn_kend"), u + 1)
                    turn_keys(1, u)
                if u > 0:
                    state(1, u - 1)
            head_scales("hn1")
            projection_out("oc", (HH, HL_O))

            rms("n3")
            pe.wait_ge(S("router_in"), 32)
            b = open_bank("act")
            for k in range(KD):
                pe.wait_ge(S("n3_h"), k + 1)
                ins = mm(b[0:NE, 0:NT], wrt[:, k, :], hT[:, k, :], start=(k == 0), stop=(k == KD - 1))
                if k < NSPLIT:
                    ins.then_inc(S("unit_used"), 1)
            close_bank("act", ins, "logit_rows")
            after_empty(pe, "logit_rows")
            b = open_bank("dve")
            for i, (t0, tn) in enumerate(BLK):
                ins = nc.tensor.transpose(b[0:tn, i * NE:(i + 1) * NE], LGT[:, t0:t0 + tn], ident[0:NE, 0:NE])
            close_bank("dve", ins, "logits")
            for i, (t0, tn) in enumerate(BLK):
                for g in range(2):
                    b = open_bank("act")
                    for k in range(4):
                        ins = nc.tensor.transpose(b[0:tn, k * P:(k + 1) * P], hT[:, 4 * g + k, t0:t0 + tn], ident)
                    close_bank("act", ins, ("hn", i, g))
            pe.wait_ge(S("chosen"), 1)
            b = open_bank("dve")
            for i, (t0, tn) in enumerate(BLK):
                for j in range(i):
                    mm(b[0:tn, i * NE:(i + 1) * NE], ones[:, 0:tn], SELM[:, j, :], start=(j == 0), stop=False)
                mm(b[0:tn, i * NE:(i + 1) * NE], C("tri")[0:tn, 0:tn], SELM[0:tn, i, :], start=(i == 0), stop=True)
            for i, (t0, tn) in enumerate(BLK):
                ins = mm(b[:, 3 * NE:4 * NE], ones[0:tn, :], SELM[0:tn, i, :], start=(i == 0), stop=(i == 2))
            close_bank("dve", ins, "ranks")

            after_empty(pe, "ranks")
            after_empty(pe, ("hn", 2, 1))

            def gather():
                for g in range(2):
                    for m in range(4):
                        at = (4 * g + m) * P
                        for i, (t0, tn) in enumerate(BLK):
                            for part in (HNH, HNL):
                                ins = mm(banks[6 + g][:, m * CAP:(m + 1) * CAP], part[0:tn, i, at:at + P],
                                         SE[0:tn, i, :], start=(i == 0 and part is HNH), stop=(i == 2 and part is HNL))
                    ins.then_inc(S("misc_full"), 1)

            def scatter(done, ms):
                pe.wait_ge(S("y_ready"), done["experts"] + 1)
                for m in ms:
                    at = slice(m * P, (m + 1) * P)
                    pe.wait_ge(S("misc_done"), done["misc"] + m + 1)
                    mm(banks[6 + m % 2][:, 0:NT], YH[:, at], STH[:, :], start=True, stop=False)
                    ins = mm(banks[6 + m % 2][:, 0:NT], YL[:, at], STH[:, :], start=False, stop=True)
                    ins.then_inc(S("misc_full"), 1)

            pe.wait_ge(S("rounds_known"), 1)
            rounds = pe.value_load(NIT[0:1, 0:1], min_val=NE, max_val=3 * NE)
            pe.wait_ge(S("sel_ready"), 1)
            pe.wait_ge(S("hn_split"), 3)
            gather()
            with pe.Fori(0, rounds) as it:
                def gate_up(c):
                    for half in range(2):
                        p = turn_of[("ab"[half], c)]
                        pe.wait_ge(S("unit_split"), it * NU + p + 1)
                        if c >= 2 and half == 0:
                            pe.wait_ge(S("a_ready"), it * NFC + c - 1)
                        if c == 0 and half == 0:
                            pe.wait_ge(S("misc_done"), it * 10 + 2)
                        wh, wl = [w[p % NSPLIT][:, :].rearrange("p (k n) -> p k n", n=512) for w in (WH, WL)]
                        for q in range(4):
                            k = 4 * half + q
                            b = banks[c % 2][:, :]
                            ins = product3(b, (XGH[:, k, :], XGL[:, k, :]), (wh[:, q, :], wl[:, q, :]),
                                           k == 0, k == KD - 1)
                        ins.then_inc(S("unit_used"), 1)

                def turn(c):
                    pe.wait_ge(S("a_ready"), it * NFC + c + 1)
                    if c >= 2:
                        pe.wait_ge(S("t_copied"), it * 12 + c - 1)
                    for j in range(2):
                        ins = nc.tensor.transpose(banks[4 + c % 2][:, j * P:(j + 1) * P], AN[:, c % 2, j * P:(j + 1) * P],
                                                  ident)
                    ins.then_inc(S("t_full"), 1)

                def turn_selection():
                    t = NFC
                    pe.wait_ge(S("t_copied"), it * 12 + t - 1)
                    for i, (t0, tn) in enumerate(BLK):
                        ins = nc.tensor.transpose(banks[4 + t % 2][:, t0:t0 + tn], SGE[0:tn, i, :], ident[0:tn, 0:tn])
                    ins.then_inc(S("t_full"), 1)

                def down(c):
                    p = turn_of[("d", c)]
                    pe.wait_ge(S("unit_split"), it * NU + p + 1)
                    pe.wait_ge(S("t_copied"), it * 12 + c + 1)
                    wh, wl = [w[p % NSPLIT][:, :].rearrange("p (j n) -> p j n", n=D) for w in (WH, WL)]
                    for j in range(2):
                        ah, al = [A_[:, c % 2, j * P:(j + 1) * P] for A_ in (ATH, ATL)]
                        for g in range(2):
                            b, at = banks[2 + g][:, :], slice(g * 512, (g + 1) * 512)
                            first, last = c == 0 and j == 0, c == NFC - 1 and j == 1
                            ins = product3(b, (ah, al), (wh[:, j, at], wl[:, j, at]), first, last)
                    ins.then_inc(S("unit_used"), 1)

                for c in range(NFC):
                    gate_up(c)
                    if 1 <= c <= 4:
                        scatter({"experts": it, "misc": it * 10}, (2 * c - 2, 2 * c - 1))
                    if c >= 1:
                        turn(c - 1)
                    if c >= 2:
                        down(c - 2)
                pe.wait_ge(S("sel_ready"), it + 2)
                pe.wait_ge(S("misc_done"), it * 10 + 10)
                gather()
                turn(NFC - 1)
                down(NFC - 2)
                turn_selection()
                down(NFC - 1)
            scatter({"experts": rounds, "misc": rounds * 10}, range(KD))

            rms("n4")
            pe.wait_ge(S("n4_h"), KD)
            for i, (t0, tn) in enumerate(BLK):
                for g in range(2):
                    b = open_bank("act")
                    for k in range(4):
                        ins = nc.tensor.transpose(b[0:tn, k * P:(k + 1) * P], hT[:, 4 * g + k, t0:t0 + tn], ident)
                    close_bank("act", ins, ("yn", i, g))

        @block.sync
        def _(sp):
            x_p = A["x_prompt"][0].rearrange("(i p) d -> p i d", p=P)
            x_s = A["x_sample"].rearrange("b t d -> (b t) d")
            sp.dma_start(XN[:, 0:2, :], x_p).then_inc(S("x_in"), 16)
            sp.dma_start(XN[0:SMP, 2, :], x_s).then_inc(S("x_in"), 16)

            def load_dense(n):
                if n >= DSTAGE:
                    sp.wait_ge(S("dense_split"), n - DSTAGE + 1)
                key, c, half = plan[n]
                v = unit_view(n, DST)
                sem = dense_landed[n % DSTAGE]
                if key == "ffn":
                    at = slice(c * FC + half * P, c * FC + half * P + P)
                    sp.dma_start(v[:, :, 0:P], w_fg[:, :, at]).then_inc(sem, 16)
                    sp.dma_start(v[:, :, P:2 * P], w_fu[:, :, at]).then_inc(sem, 16)
                elif key == "fd":
                    src = w_fd[:, half * (FT // 2):(half + 1) * (FT // 2), c * P:(c + 1) * P]
                    sp.dma_start(v[:, 0:5, :], src[:, 0:5, :]).then_inc(sem, 16)
                    sp.dma_start(v[:, 5:11, :], src[:, 5:11, :]).then_inc(sem, 16)
                else:
                    at = slice(c * 512 + half * 256, c * 512 + (half + 1) * 256)
                    src = {"ab": w_ab, "oab": w_oab, "c": w_c, "oc": w_oc}[key][:, :, at]
                    sp.dma_start(v[:, 0:4, :], src[:, 0:4, :]).then_inc(sem, 16)
                    sp.dma_start(v[:, 4:8, :], src[:, 4:8, :]).then_inc(sem, 16)

            for n in range(NDENSE):
                load_dense(n)

            wg = A["w_moe_gate"].rearrange("o e (k p) n -> p (o e) k n", p=P)
            wu = A["w_moe_up"].rearrange("o e (k p) n -> p (o e) k n", p=P)
            wd = A["w_moe_down"].rearrange("o e (k p) n -> p (o e) k n", p=P)

            def load_unit(e, p):
                kind, c = UNITS[p]
                sem = stage_landed[p % NSTAGE]
                if kind == "d":
                    v = STAGE[:, p % NSTAGE, :].rearrange("p (j n) -> p j n", n=D)
                    for j in range(2):
                        src = wd[:, bass.ds(e, 1), 2 * c + j:2 * c + j + 1, :].rearrange("p o k n -> p (o k) n")
                        sp.dma_start(v[:, j:j + 1, :], src).then_inc(sem, 16)
                else:
                    v = STAGE[:, p % NSTAGE, :].rearrange("p (k n) -> p k n", n=512)
                    k = 4 * "ab".index(kind)
                    for part, w in enumerate((wg, wu)):
                        src = w[:, bass.ds(e, 1), k:k + 4, c * FC:(c + 1) * FC].rearrange("p o k n -> p (o k) n")
                        sp.dma_start(v[:, :, part * FC:(part + 1) * FC], src).then_inc(sem, 16)

            def load_expert(e, done):
                for p in range(NU):
                    if p >= NSTAGE:
                        sp.wait_ge(S("unit_split"), p - NSTAGE + 1 if done is None else done + (p - NSTAGE + 1))
                    elif done is not None:
                        before = max(range(p, NU, NSTAGE))
                        sp.wait_ge(S("unit_split"), done + (before + 1 - NU))
                    load_unit(e, p)

            for i in range(NST):
                sp.wait_ge(S(f"state_out_{i}"), 16 * len(range(i, KD, NST)) * 2)
            after_fill(sp, ("oc", KD - 1))
            load_expert(0, None)
            sp.wait_ge(S("rounds_known"), 1)
            rounds = sp.value_load(NIT[0:1, 0:1], min_val=NE, max_val=3 * NE)
            with sp.Fori(1, rounds) as it:
                e = it & (NE - 1)
                sp.compute_val(e)
                load_expert(e, it * NU)

            y_p = O["y_prompt"][0].rearrange("(i p) d -> p i d", p=P)
            y_s = O["y_sample"].rearrange("b t d -> (b t) d")
            after_empty(sp, ("yn", 1, 1))
            sp.dma_start(y_p, YN[:, 0:2, :]).then_inc(S("y_out"), 16)
            after_empty(sp, ("yn", 2, 1))
            sp.dma_start(y_s, YN[0:SMP, 2, :]).then_inc(S("y_out"), 16)
            sp.wait_ge(S("y_out"), 32)

        @block.scalar
        def _(act):
            tick = {"n": 0}
            act_step = S("act_step")

            def step(ins):
                tick["n"] += 1
                ins.then_inc(act_step, 1)
                return tick["n"]

            def take(name):
                after_fill(act, name)
                kind, n = ticket[name]
                assert kind == "act"
                return bank_of("act", n)

            def free(ins):
                ins.then_inc(emptied["act"], 1)

            fn = nc.scalar.activation

            act.dma_start(cst[:, 0:NFIRST], A["cst"][:, 0:NFIRST]).then_inc(S("const_in"), 16)
            for name, key, nrows in (("ln_mix", "ln_mix", 16), ("ln_ffn", "ln_ffn", 16), ("ln_final", "ln_final", 8),
                                     ("conv_w", "conv_w_ab", 32), ("conv_b", "conv_b_ab", 8), ("ret_gn", "ret_gn", 4),
                                     ("ml_gn", "ml_gn", 4), ("hg_lower", "hg_lower", 16), ("hg_gn", "hg_gn", 8)):
                a = A[key]
                pattern = {1: "(k p) -> k p", 2: "a (k p) -> (a k) p", 3: "o a (k p) -> (o a k) p"}[len(a.shape)]
                act.dma_start(PN[PRM[name]:PRM[name] + nrows, :], a.rearrange(pattern, p=P)).then_inc(S("prm_in"), 16)
            act.dma_start(CN[0:24, :], A["state_conv"][0].rearrange("b j c -> (b j) c")).then_inc(S("carry_in"), 16)
            act.dma_start(NN[0:32, :], A["state_mlstm_n"][0].rearrange("b h k -> (b h) k")).then_inc(S("carry_in"), 16)
            act.dma_start(wgate[:, :, :], w_ab[:, :, 4096:4104]).then_inc(S("wgate_in"), 16)
            act.dma_start(gbias[:, :], A["b_gates_ab"][0].rearrange("(r h) -> h r", r=2),
                          allow_slow_non_contiguous=True).then_inc(S("rows_in"), 16)
            act.dma_start(mrow[:, :], A["state_mlstm_m"][0].rearrange("b h -> h b"),
                          allow_slow_non_contiguous=True).then_inc(S("rows_in"), 16)
            act.dma_start(wrt[:, :, :], A["w_router"][0].rearrange("(k p) e -> p k e", p=P)).then_inc(S("router_in"), 16)
            act.dma_start(brt[:, :], A["b_router"].rearrange("o e -> e o"),
                          allow_slow_non_contiguous=True).then_inc(S("router_in"), 16)

            split = iter(range(NDENSE))

            def split_dense():
                n = next(split, None)
                if n is None:
                    return
                act.wait_ge(dense_landed[n % DSTAGE], 32 * (n // DSTAGE + 1))
                if n >= DSPLIT:
                    act.wait_ge(*unit_read[n - DSPLIT])
                fn(unit_flat(n, DWH), unit_flat(n, DST), ACT.Copy).then_inc(S("dense_hi"), 1)

            def high(tag, src, scaled=None):
                for k in range(KD):
                    if scaled is None:
                        act.wait_ge(S(tag + "_value"), k + 1)
                    else:
                        after_empty(act, (scaled, "scale", k))
                    fn(HH[:, k, :], src[:, k, :], ACT.Copy).then_inc(S(tag + "_hi"), 1)

            act.dma_start(cst[:, NFIRST:], A["cst"][:, NFIRST:]).then_inc(S("tables_in"), 16)

            def squares(tag, ready, ks=range(KD)):
                for k in ks:
                    ready(k)
                    fn(SQF[tag][:, k, :], xT[:, k, :], ACT.Square).then_inc(S(tag + "_squares"), 1)

            def root(tag):
                b = take((tag, "ms"))
                free(fn(RSQ, b[:, 0:NT], ACT.Sqrt, bias=C("eps")))

            RSQ = rsq[:, :]

            squares("n0", lambda k: after_empty(act, ("xT", k)))
            root("n0")
            split_dense()
            free(fn(prm[:, :], take("prm")[:, 0:NPRM], ACT.Copy))
            high("n0", OR)
            b = take("carry")
            act.wait_ge(S("history_zero"), 1)
            hist = XC[:, :, SX:XW].rearrange("p k (b t) -> p k b t", t=3 + TS)[:, :, :, 0:3]
            for k in range(KD):
                fn(hist[:, k], b[:, 24 * k:24 * k + 24].rearrange("p (b j) -> p b j", j=3), ACT.Copy)
            free(fn(NS0, b[:, 192:224], ACT.Copy))
            split_dense()
            act.wait_ge(S("wgate_in"), 16)
            fn(WGH[:, :, :], wgate[:, :, :], ACT.Copy).then_inc(S("wgate_hi"), 1)

            def conv_silu(k):
                act.wait_ge(S("conv_sum"), k + 1)
                dst = (Q if k < 4 else K)[:, H4 + k % 4, :]
                fn(dst[:, 0:TP], CV[:, k, 0:TP], ACT.Silu)
                src = CV[:, k, TP:CW].rearrange("p (b t) -> p b t", t=3 + TS)[:, :, 3:3 + TS]
                fn(dst[:, TP:NT].rearrange("p (b t) -> p b t", t=TS), src, ACT.Silu).then_inc(S("conv_silu"), 1)

            for c in AB_ORDER:
                for half in range(2):
                    for h in (2 * half, 2 * half + 1) if c not in (2, 6) else ():
                        b = take(("ab", c, h))
                        if c in (4, 5):
                            k = 4 * (c - 4) + h
                            fn(XC[:, k, 3:SX], b[:, 0:TP], ACT.Copy)
                            new = XC[:, k, SX:XW].rearrange("p (b t) -> p b t", t=3 + TS)[:, :, 3:3 + TS]
                            free(fn(new, b[:, TP:NT].rearrange("p (b t) -> p b t", t=TS), ACT.Copy))
                        elif c in (0, 1):
                            free(fn((Q, K)[c][:, h, :], b[:, 0:NT], ACT.Copy))
                        elif c == 3:
                            free(fn(G[:, h, :], b[:, 0:NT], ACT.Silu))
                        else:
                            free(fn(G[:, H4 + h, :], b[:, 0:NT], ACT.Sigmoid))
                    split_dense()
                    if c in (1, 2):
                        for k in range(2):
                            conv_silu(4 * (c == 2) + 2 * half + k)
                if c == 5:
                    act.wait_ge(S("rows_in"), 32)
                    free(fn(I_R, take(("gate", 0))[0:H4, 0:NT], ACT.Identity, bias=gbias[:, 0:1]))
                    free(fn(Z_R, take(("gate", 1))[0:H4, 0:NT], ACT.Identity, bias=gbias[:, 1:2]))
                    act.wait_ge(S("gate_abs"), 1)
                    n = step(fn(L_R, T_R, ACT.Exp, scale=-1.0))
                    act.wait_ge(act_step, n)
                    fn(L_R, L_R, ACT.Ln, bias=1.0).then_inc(S("gate_ln"), 1)
                    act.wait_ge(S("gate_exps_in"), 1)
                    fn(wprow[:, :], wprow[:, :], ACT.Exp).then_inc(S("gate_exps"), 1)
                    fn(WE_R, WE_R, ACT.Exp).then_inc(S("gate_exps"), 1)
            b = take("cols")
            for i, (t0, tn) in enumerate(BLK):
                ins = fn(SRC[0:tn, i].rearrange("p r h -> p (r h)"), b[0:tn, 8 * i:8 * i + 8], ACT.Copy)
            free(ins)
            for g in range(2):
                free(fn(CO[:, g * 512:(g + 1) * 512], take(("conv_out", g))[0:27, :], ACT.Copy))
            after_empty(act, ("conv_out", 1))
            act.dma_start(O["conv_p"][0, 0], CO[0:3, :]).then_inc(S("stores"), 16)
            act.dma_start(O["conv_s"][0].rearrange("b j c -> (b j) c"), CO[3:27, :]).then_inc(S("stores"), 16)

            def keys(layer, u, scale):
                b = take(("kn", layer, u))
                for i, (t0, tn) in enumerate(BLK):
                    dst, src = KN[0:tn, u % 2, i, :], b[0:tn, i * P:(i + 1) * P]
                    ins = fn(dst, src, ACT.Copy) if scale is None else fn(dst, src, ACT.Copy, scale=scale(i, tn))
                free(ins)

            def prompt_state(layer, u):
                b = take(("sp", layer, u))
                if u + 8 * layer >= 2:
                    act.wait_ge(S(f"sp_stored_{u % 2}"), 16 * ((u + 8 * layer) // 2))
                ins = fn(SPO[:, u % 2, :], b[:, 0:DH], ACT.Copy)
                if layer == 0 and u >= H4:
                    ins = fn(NRAW[:, u - H4, :], b[:, DH:DH + 9], ACT.Copy)
                free(ins)
                out = O["hg_p"] if layer else O["ret_p"] if u < H4 else O["mc_p"]
                after_empty(act, ("sp", layer, u))
                act.dma_start(out[0, 0, u if layer else u % H4], SPO[:, u % 2, :]).then_inc(S(f"sp_stored_{u % 2}"), 16)

            kdec = C("kdec").rearrange("p (i h) -> p i h", h=H4)

            def centered(u):
                b = take(("cen", u))
                fn(OR[:, u, :], b[:, 0:NT], ACT.Copy)
                free(fn(SQH[:, u, :], b[:, 0:NT], ACT.Square))

            for u in range(KD + 1):
                if H4 <= u < KD:
                    b = take(("em", u))
                    if u >= H4 + 2:
                        after_empty(act, ("den", u - 2))
                    free(fn(EM[:, u % 2, :], b[:, 0:NT], ACT.Exp, scale=-1.0))
                    after_empty(act, ("bc", u))
                    h = u - H4
                    fn(WB[:, 0:TP], WB[:, 0:TP], ACT.Exp, bias=SRC[:, 0, 0, h:h + 1])
                    fn(WB[:, TP:384], WB[:, TP:384], ACT.Exp, bias=SRC[:, 1, 0, h:h + 1])
                    fn(WB[0:SMP, 384:448], WB[0:SMP, 384:448], ACT.Exp,
                       bias=SRC[0:SMP, 2, 0, h:h + 1]).then_inc(S("w_exp"), 1)
                if u < KD:
                    if u < H4:
                        keys(0, u, lambda i, tn: kdec[0:tn, i, u:u + 1])
                    else:
                        keys(0, u, lambda i, tn: SRC[0:tn, i, 1, u - H4:u - H4 + 1])
                if u > 0:
                    prompt_state(0, u - 1)
                if u > 1:
                    centered(u - 2)
            free(fn(NTO[:, :], take("n_out")[0:36, 0:P], ACT.Copy))
            after_empty(act, "n_out")
            act.dma_start(O["mn_s"][0].rearrange("b h k -> (b h) k"), NTO[0:32, :]).then_inc(S("stores"), 16)
            act.dma_start(O["mn_p"][0, 0], NTO[32:36, :]).then_inc(S("stores"), 16)
            act.dma_start(O["mm_s"][0].rearrange("b h -> h b"),
                          MT_R[:, TP:NT].rearrange("h (b t) -> h b t", t=TS)[:, :, TS - 1:TS].rearrange("h b o -> h (b o)"),
                          allow_slow_non_contiguous=True).then_inc(S("stores"), 16)
            act.dma_start(O["mm_p"][0].rearrange("b h -> h b"), MT_R[:, TP - 1:TP],
                          allow_slow_non_contiguous=True).then_inc(S("stores"), 16)

            def head_roots(tag):
                free(fn(rsq[0:KD, :], take((tag, "var"))[0:KD, 0:NT], ACT.Sqrt, bias=C("eps", KD)))

            def projected_out(kind, tag):
                for u in range(4):
                    split_dense()
                    squares(tag, lambda k: after_empty(act, (kind, k)), (2 * u, 2 * u + 1))

            centered(KD - 1)
            head_roots("hn0")
            high("mix0", OR, "hn0")
            projected_out("oab", "n1")
            root("n1")
            high("n1", OR)
            for f in range(FT + 1):
                if f < FT:
                    b = take(("fg", f))
                    if f >= NSG:
                        act.wait_ge(S("ff_ready"), f - NSG + 1)
                    free(fn(SG[:, f % NSG, :], b[:, 0:NT], ACT.Silu))
                if f > 0:
                    after_empty(act, ("fu", f - 1))
                    fn(FTH[:, f - 1, :], SG[:, (f - 1) % NSG, :], ACT.Copy).then_inc(S("ff_hi"), 1)
                if f < FT:
                    split_dense()
            for k in range(KD):
                split_dense()
                split_dense()
                squares("n2", lambda k: after_empty(act, ("fd", k)), (k,))
            act.wait_ge(S("lb_max"), 1)
            fn(LBT[:, 0:2, :], LBT[:, 0:2, :], ACT.Exp).then_inc(S("lb_exp"), 1)
            root("n2")
            high("n2", NX2)

            def level_exps(j):
                act.wait_ge(S("level_diff"), 8 - j)
                L = LV[j % 2]
                cols = slice(0, TP) if j >= 3 else slice(0, NT)
                fn(L[:, :, cols], L[:, :, cols], ACT.Exp).then_inc(S("level_exp"), 1)

            for c in C_ORDER:
                for half in range(2):
                    for h in (2 * half, 2 * half + 1) if c not in (4, 5) else ():
                        b = take(("c", c, h))
                        if c in (2, 3):
                            free(fn(K[:, 4 * (c - 2) + h, :], b[:, 0:NT], ACT.Sigmoid))
                        elif c in (0, 1):
                            free(fn(Q[:, 4 * c + h, :], b[:, 0:NT], ACT.Silu))
                        else:
                            free(fn(G[:, 4 * (c - 6) + h, :], b[:, 0:NT], ACT.Silu))
                    split_dense()
                    if c >= 4:
                        level_exps(7 - (2 * (c - 4) + half))
                if c == 1:
                    for h in range(HG):
                        act.wait_ge(S("forget"), h + 1)
                        fn(LV[1][:, h, :], LV[1][:, h, :], ACT.Ln).then_inc(S("forget_ln"), 1)
            act.wait_ge(S("end_diff"), 1)
            fn(LV[1][:, :, :], LV[1][:, :, :], ACT.Exp).then_inc(S("end_exp"), 1)
            fn(ES[:, :, :], CUM[:, :, TP:NT], ACT.Exp).then_inc(S("end_exp"), 1)
            for u in range(HG + 1):
                if u < HG:
                    keys(1, u, None)
                if u > 0:
                    prompt_state(1, u - 1)
                    after_empty(act, ("num", 1, u - 1))
                    fn(SQH[:, u - 1, :], OH[:, u - 1, :], ACT.Square).then_inc(S("hn1_squares"), 1)
            head_roots("hn1")
            high("mix1", OH, "hn1")
            projected_out("oc", "n3")
            root("n3")
            act.wait_ge(S("router_in"), 32)
            free(fn(LGT, take("logit_rows")[0:NE, 0:NT], ACT.Identity, bias=brt[:, 0:1]))
            for i, (t0, tn) in enumerate(BLK):
                for g in range(2):
                    free(fn(HN[0:tn, i, g * 512:(g + 1) * 512], take(("hn", i, g))[0:tn, :], ACT.Copy))
                if i == 0:
                    act.wait_ge(S("router_diff"), 1)
                    fn(GATE[:, :, :], GATE[:, :, :], ACT.Exp).then_inc(S("router_exp"), 1)
                after_empty(act, ("hn", i, 1))
                fn(HNH[0:tn, i, :], HN[0:tn, i, :], ACT.Copy).then_inc(S("hn_hi"), 1)

            act.wait_ge(S("rounds_known"), 1)
            rounds = act.value_load(NIT[0:1, 0:1], min_val=NE, max_val=3 * NE)
            act.wait_ge(S("hn_split"), 3)

            act.wait_ge(S("down_zero"), 1)

            def y_high(done):
                act.wait_ge(S("unit_used"), done * NU + NSPLIT)
                act.wait_ge(S("gates_ready"), done + 1)
                for g in range(2):
                    ins = fn(YH[:, g * 512:(g + 1) * 512], banks[2 + g][:, :], ACT.Copy, scale=GS[:, 0:1])
                ins.then_inc(S("y_hi"), 1)

            def split_high(done, p):
                act.wait_ge(stage_landed[p % NSTAGE], done * (32 * stage_uses[p % NSTAGE]) + 32 * (p // NSTAGE + 1))
                act.wait_ge(S("unit_used"), done * NU + p + 1)
                fn(WH[p % NSPLIT][:, :], STAGE[:, p % NSTAGE, :], ACT.Copy).then_inc(S("unit_hi"), 1)

            with act.Fori(0, rounds) as it:
                def silu(c):
                    act.wait_ge(S("unit_used"), it * NU + NSPLIT + turn_of[("b", c)] + 1)
                    if c >= 2:
                        act.wait_ge(S("a_ready"), it * NFC + c - 1)
                    fn(SL[:, c % 2, :], banks[c % 2][:, 0:FC], ACT.Silu).then_inc(S("silu_done"), 1)

                def turned(c):
                    act.wait_ge(S("t_full"), it * 12 + c + 1)
                    fn(ATH[:, c % 2, :], banks[4 + c % 2][:, 0:FC], ACT.Copy).then_inc(S("at_hi"), 1)

                for p in range(NSPLIT):
                    split_high(it, p)
                y_high(it)
                for p, (kind, c) in enumerate(UNITS):
                    if kind == "d" and c < NFC - 2:
                        turned(c + 1)
                    if p + NSPLIT < NU:
                        split_high(it, p + NSPLIT)
                    if kind == "b":
                        silu(c)
                    if kind == "b" and c == 1:
                        turned(0)
                    if kind == "d" and c == NFC - 3:
                        turned(NFC - 1)

            y_high(rounds)
            act.wait_ge(S("misc_done"), rounds * 10 + 10)
            squares("n4", lambda k: None)
            root("n4")
            for i, (t0, tn) in enumerate(BLK):
                for g in range(2):
                    free(fn(YN[0:tn, i, g * 512:(g + 1) * 512], take(("yn", i, g))[0:tn, :], ACT.Copy))
            act.wait_ge(S("stores"), 16 * 6)
            for r in range(2):
                act.wait_ge(S(f"sp_stored_{r}"), 16 * 8)

        @block.vector
        def _(dve):
            tick = {"n": 0}
            dve_step = S("dve_step")
            v = nc.vector

            def step(ins):
                tick["n"] += 1
                ins.then_inc(dve_step, 1)
                dve.wait_ge(dve_step, tick["n"])

            def take(name):
                after_fill(dve, name)
                kind, n = ticket[name]
                assert kind == "dve"
                return bank_of("dve", n)

            def free(ins):
                ins.then_inc(emptied["dve"], 1)

            split = iter(range(NDENSE))

            def split_dense():
                n = next(split, None)
                if n is None:
                    return
                dve.wait_ge(S("dense_hi"), n + 1)
                v.tensor_tensor(unit_flat(n, DWL), unit_flat(n, DST), unit_flat(n, DWH).bitcast(F32),
                                ALU.subtract).then_inc(S("dense_split"), 1)

            def low(tag, k, src, lo):
                dve.wait_ge(S(tag + "_hi"), k + 1)
                v.tensor_tensor(lo[:, k, :], src[:, k, :], HH[:, k, :].bitcast(F32), ALU.subtract).then_inc(
                    S(tag + "_h"), 1)

            def normed(tag, gain, row, dst, lo=None, between=lambda: None):
                after_empty(dve, (tag, "ms"))
                step(v.reciprocal(rsq[:, :], rsq[:, :]))
                between()
                for k in range(KD + 1):
                    if k < KD:
                        v.scalar_tensor_tensor(out=dst[:, k, :], in0=xT[:, k, :], scalar=prow(gain, row + k),
                                               in1=rsq[:, :], op0=ALU.mult, op1=ALU.mult).then_inc(
                            S(tag + ("_h" if lo is None else "_value")), 1)
                    if k > 0 and lo is not None:
                        low(tag, k - 1, dst, lo)

            def add_to_x(name, k):
                b = take(name)
                free(v.tensor_tensor(xT[:, k, :], xT[:, k, :], b[:, 0:NT], ALU.add))

            for k in range(KD):
                free(v.tensor_copy(xT[:, k, :], take(("xT", k))[:, 0:NT]))

            def first_weights():
                split_dense()
                after_empty(dve, "prm")

            normed("n0", "ln_mix", 0, OR, HL_A, first_weights)
            split_dense()

            def values(layer, c, half):
                at = 512 * c + 256 * half
                for i, (t0, tn) in enumerate(BLK):
                    free(v.tensor_copy(V[0:tn, i, at:at + 256], take((("V", layer, c), half, i))[0:tn, 0:256]))

            for n in range(4):
                split_dense()
                if n == 0:
                    dve.wait_ge(S("wgate_hi"), 1)
                    v.tensor_tensor(WGL[:, :, :], wgate[:, :, :], WGH[:, :, :].bitcast(F32),
                                    ALU.subtract).then_inc(S("wgate_split"), 1)
            after_empty(dve, ("gate", 1))
            v.scalar_tensor_tensor(out=T_R, in0=Z_R, scalar=-1.0, in1=Z_R, op0=ALU.mult,
                                   op1=ALU.max).then_inc(S("gate_abs"), 1)
            dve.wait_ge(S("gate_ln"), 1)
            dve.wait_ge(S("tables_in"), 16)
            step(v.scalar_tensor_tensor(out=Z_R, in0=Z_R, scalar=0.0, in1=L_R, op0=ALU.min, op1=ALU.subtract))
            step(v.tensor_tensor_scan(B_R, C("reset", H4), Z_R, 0.0, ALU.mult, ALU.add))
            step(v.tensor_tensor(SRC_R, I_R, B_R, ALU.subtract))
            step(v.tensor_tensor_scan(T_R, C("minrow", H4), SRC_R, -3e38, ALU.min, ALU.max))
            dve.wait_ge(S("rows_in"), 32)
            seq = lambda row: row[:, TP:NT].rearrange("h (b t) -> h b t", t=TS)
            m0 = mrow[:, :].unsqueeze(2).to_broadcast([H4, NB, TS])
            step(v.tensor_tensor(seq(T_R), seq(T_R), m0, ALU.max))
            step(v.tensor_scalar(NGM_R, T_R, -1.0, None, ALU.mult))
            v.tensor_tensor(MT_R, B_R, T_R, ALU.add)
            wp3 = wprow[:, :].rearrange("h (b t) -> h b t", t=TS)
            v.tensor_tensor(wp3, seq(NGM_R), m0, ALU.add)
            v.tensor_tensor(WE_R[:, 0:TP], SRC_R[:, 0:TP], NGM_R[:, TP - 1:TP].to_broadcast([H4, TP]), ALU.add)
            v.tensor_tensor(seq(WE_R), seq(SRC_R), seq(NGM_R)[:, :, TS - 1:TS].to_broadcast([H4, NB, TS]),
                            ALU.add).then_inc(S("gate_exps_in"), 1)
            after_empty(dve, ("ab", 5, 3))
            after_empty(dve, "carry")

            def conv(k):
                cw = lambda j: prow("conv_w", j * KD + k)
                step(v.tensor_scalar(CV[:, k, :], XC[:, k, 0:CW], cw(0), prow("conv_b", k), ALU.mult, ALU.add))
                for j in range(1, NCONV):
                    ins = v.scalar_tensor_tensor(out=CV[:, k, :], in0=XC[:, k, j:j + CW], scalar=cw(j), in1=CV[:, k, :],
                                                 op0=ALU.mult, op1=ALU.add)
                    if j < NCONV - 1:
                        step(ins)
                    else:
                        ins.then_inc(S("conv_sum"), 1)

            def rope(r):
                X4 = (Q, K)[r][:, 0:H4, :]
                after_empty(dve, ("ab", r, 3))
                wide = lambda ap, n: ap.unsqueeze(1).to_broadcast([n, H4, NT])
                sin, cos = C("sin"), C("cos")
                if r == 1:
                    dve.wait_ge(S("rope_done"), 1)
                v.tensor_tensor(ROT[64:128], X4[0:64], wide(sin[0:64, :], 64), ALU.mult)
                step(v.tensor_tensor(ROT[0:64], X4[64:128], wide(sin[64:128, :], 64), ALU.mult))
                step(v.tensor_tensor(X4, X4, wide(cos, P), ALU.mult))
                v.tensor_tensor(X4, X4, ROT, ALU.add).then_inc(S("rope_done"), 1)

            for c in (6, 0, 1, 2, 3, 7):
                for half in range(2):
                    if c == 6:
                        values(0, 1, half)
                    if c == 2:
                        values(0, 0, half)
                    split_dense()
                    if c in (6, 0):
                        for k in range(2):
                            conv(4 * (c == 0) + 2 * half + k)
                    if c == 1 and half == 0:
                        rope(0)
                    if c == 2 and half == 0:
                        rope(1)
            dve.wait_ge(S("rope_done"), 2)

            def new_states(layer, u, scale):
                slot = ST[:, u % NST]
                for g in range(2):
                    b = take(("ss", layer, u, g))
                    for s in range(4):
                        q = 4 * g + s
                        ins = v.scalar_tensor_tensor(out=slot[:, q, :], in0=slot[:, q, :], scalar=scale(q),
                                                     in1=b[:, s * DH:(s + 1) * DH], op0=ALU.mult, op1=ALU.add)
                    free(ins)

            decay = C("decay").rearrange("p (h n) -> p h n", n=320)
            qdec = C("qdec").rearrange("p (h n) -> p h n", n=SMP)
            mmask = C("mmask")
            for u in range(KD + 1):
                if H4 <= u < KD:
                    b = take(("bc", u))
                    v.tensor_tensor(WB[:, 0:P], b[:, 0:P], mmask[:, 0:P], ALU.add)
                    v.tensor_copy(WB[:, P:TP], b[:, P:TP])
                    v.tensor_tensor(WB[:, TP:384], b[:, P:TP], mmask[:, 0:P], ALU.add)
                    v.tensor_tensor(WB[0:SMP, 384:448], b[0:SMP, TP:NT], mmask[0:SMP, P:192], ALU.add)
                    free(v.tensor_copy(WPS[:, u % 2, :], b[:, NT:NT + SMP]))
                    after_empty(dve, ("bc", u))
                if u > 0:
                    w = u - 1
                    b = take(("num", 0, w))
                    if w < H4:
                        free(v.tensor_copy(OR[:, w, :], b[:, 0:NT]))
                    else:
                        free(v.tensor_copy(OR[:, w, :], b[:, 0:NT]))
                        d = take(("den", w))
                        after_empty(dve, ("em", w))
                        step(v.scalar_tensor_tensor(out=rsq[:, :], in0=d[:, 0:NT], scalar=-1.0, in1=EM[:, w % 2, :],
                                                    op0=ALU.mult, op1=ALU.max))
                        free(v.tensor_tensor(rsq[:, :], rsq[:, :], d[:, 0:NT], ALU.max))
                        after_empty(dve, ("den", w))
                        step(v.reciprocal(rsq[:, :], rsq[:, :]))
                        step(v.tensor_tensor(OR[:, w, :], OR[:, w, :], rsq[:, :], ALU.mult))
                        after_empty(dve, ("ab", 7, w - H4))
                        v.tensor_tensor(OR[:, w, :], OR[:, w, :], G[:, w, :], ALU.mult).then_inc(S("o_mlstm"), 1)
                if u < KD:
                    if u == H4:
                        dve.wait_ge(S("keys_scaled"), 1)
                    if u < H4:
                        v.tensor_tensor(QE[:, u % 2, :], Q[:, u, TP:NT], qdec[:, u, :], ALU.mult).then_inc(S("qe0"), 1)
                        b = take(("sc", 0, u))
                        pb = PB[:, u % 2, :]
                        v.tensor_tensor(pb[:, 0:TP], b[:, 0:TP], decay[:, u, 0:TP], ALU.mult)
                        v.tensor_tensor(pb[:, TP:384], b[:, TP:384], decay[:, u, 0:P], ALU.mult)
                        free(v.tensor_tensor(pb[0:SMP, 384:448], b[0:SMP, 384:448], decay[0:SMP, u, TP:320], ALU.mult))
                    else:
                        h = u - H4
                        v.tensor_tensor(QE[:, u % 2, :], Q[:, u, TP:NT], WPS[:, u % 2, :], ALU.mult).then_inc(S("qe0"), 1)
                        dve.wait_ge(S("w_exp"), h + 1)
                        b = take(("sc", 0, u))
                        pb = PB[:, u % 2, :]
                        v.tensor_tensor(pb[:, 0:384], b[:, 0:384], WB[:, 0:384], ALU.mult)
                        free(v.tensor_tensor(pb[0:SMP, 384:448], b[0:SMP, 384:448], WB[0:SMP, 384:448], ALU.mult))
                        n0 = NS0.rearrange("p (b h) -> p b h", h=H4)[:, :, h:h + 1]
                        wps = WPS[:, u % 2, :].rearrange("p (b t) -> p b t", t=TS)
                        qe = QE[:, u % 2, :].rearrange("p (b t) -> p b t", t=TS)
                        no = NOUT[:, 0:32].rearrange("p (b h) -> p b h", h=H4)[:, :, h:h + 1]
                        step(v.tensor_copy(MDEC[:, u % 2, :].unsqueeze(2), wps[:, :, TS - 1:TS]))
                        v.tensor_tensor(no, n0, MDEC[:, u % 2, :].unsqueeze(2), ALU.mult)
                        dve.wait_ge(S("qe0"), u + 1)
                        v.tensor_tensor(wps, qe, n0.to_broadcast([P, NB, TS]), ALU.mult).then_inc(S("qn"), 1)
                if u > 0:
                    w = u - 1
                    if w < H4:
                        new_states(0, w, lambda q: GAMMA[w] ** TS)
                    else:
                        new_states(0, w, lambda q: MDEC[:, w % 2, q:q + 1])
                        after_empty(dve, ("sp", 0, w))
                        h = w - H4
                        no = NOUT[:, 0:32].rearrange("p (b h) -> p b h", h=H4)[:, :, h:h + 1]
                        v.tensor_tensor(no, no, NRAW[:, h, 1:9].unsqueeze(2), ALU.add)
                        ins = v.tensor_copy(NOUT[:, 32 + h:33 + h], NRAW[:, h, 0:1])
                        if w == KD - 1:
                            ins.then_inc(S("n_out"), 1)
                if 1 < u < H4 + 2:
                    w = u - 2
                    after_empty(dve, ("cen", w))
                    v.scalar_tensor_tensor(out=OR[:, w, :], in0=OR[:, w, :], scalar=prow("ret_gn", w), in1=G[:, w, :],
                                           op0=ALU.mult, op1=ALU.mult).then_inc(S("gated0"), 1)
            dve.wait_ge(S("gated0"), H4)

            def mix(src, tag, gain, lo):
                out = "mix0" if tag == "hn0" else "mix1"
                after_empty(dve, (tag, "var"))
                v.reciprocal(rsq[0:KD, :], rsq[0:KD, :]).then_inc(S(tag + "_scales"), 1)
                for u in range(KD + 1):
                    if u < KD:
                        b = take((tag, "scale", u))
                        if gain(u) is None:
                            ins = v.tensor_tensor(src[:, u, :], src[:, u, :], b[:, 0:NT], ALU.mult)
                        else:
                            ins = v.scalar_tensor_tensor(out=src[:, u, :], in0=b[:, 0:NT], scalar=gain(u),
                                                         in1=src[:, u, :], op0=ALU.mult, op1=ALU.mult)
                        free(ins)
                    if u > 0:
                        low(out, u - 1, src, lo)

            def projected_out(kind):
                for u in range(4):
                    for k in (2 * u, 2 * u + 1):
                        add_to_x((kind, k), k)
                    split_dense()

            mix(OR, "hn0", lambda u: None if u < H4 else prow("ml_gn", u - H4), HL_A)
            projected_out("oab")
            normed("n1", "ln_ffn", 0, OR, HL_A)
            for f in range(FT + 1):
                if f < FT:
                    b = take(("fu", f))
                    after_empty(dve, ("fg", f))
                    free(v.tensor_tensor(SG[:, f % NSG, :], SG[:, f % NSG, :], b[:, 0:NT], ALU.mult))
                if f == FT // 2:
                    for i in range(NST):
                        dve.wait_ge(S(f"state_out_{i}"), 16 * len(range(i, KD, NST)))
                if f > 0:
                    dve.wait_ge(S("ff_hi"), f)
                    v.tensor_tensor(FTL[:, f - 1, :], SG[:, (f - 1) % NSG, :], FTH[:, f - 1, :].bitcast(F32),
                                    ALU.subtract).then_inc(S("ff_ready"), 1)
                if f < FT:
                    split_dense()
            for k in range(KD):
                split_dense()
                add_to_x(("fd", k), k)
                split_dense()

            bound = prm[:, PRM["hg_lower"]:PRM["hg_lower"] + 16].rearrange("p (a b) -> p a b", b=8)
            step(v.tensor_tensor(LBT[:, 2, :], bound[:, 0, :], bound[:, 1, :], ALU.max))
            v.tensor_tensor(LBT[:, 0, :], bound[:, 0, :], LBT[:, 2, :], ALU.subtract)
            v.tensor_tensor(LBT[:, 1, :], bound[:, 1, :], LBT[:, 2, :], ALU.subtract).then_inc(S("lb_max"), 1)
            dve.wait_ge(S("lb_exp"), 1)
            step(v.tensor_tensor(LBT[:, 2, :], LBT[:, 0, :], LBT[:, 1, :], ALU.add))
            step(v.reciprocal(LBT[:, 2, :], LBT[:, 2, :]))
            step(v.tensor_tensor(LB, LBT[:, 1, :], LBT[:, 2, :], ALU.mult))
            step(v.tensor_scalar(OMLB, LB, -1.0, 1.0, ALU.mult, ALU.add))
            dve.wait_ge(S("stores"), 16 * 6)
            normed("n2", "ln_mix", 8, NX2, HL_C)

            def forget(h):
                after_empty(dve, ("c", 2 + h // 4, h % 4))
                v.tensor_scalar(LV[1][:, h, :], K[:, h, :], OMLB[:, h:h + 1], LB[:, h:h + 1], ALU.mult,
                                ALU.add).then_inc(S("forget"), 1)
                dve.wait_ge(S("forget"), h + 1)
                v.tensor_scalar(K[:, h, :], LV[1][:, h, :], -1.0, 1.0, ALU.mult, ALU.add).then_inc(S("hgrn_k"), 1)

            def level_differences(j):
                L = LV[j % 2]
                ls, lt, _ = halves(L, j)
                cs, ct, ref = halves(CUM, j)
                v.tensor_tensor(lt, ct, ref.to_broadcast(list(ct.shape)), ALU.subtract)
                v.tensor_tensor(ls, ref.to_broadcast(list(cs.shape)), cs, ALU.subtract).then_inc(S("level_diff"), 1)

            def level_queries(j):
                L = LV[j % 2]
                _, lt, _ = halves(L, j)
                _, qt, _ = halves(Q, j)
                dve.wait_ge(S("level_exp"), 8 - j)
                v.tensor_tensor(lt, lt, qt, ALU.mult).then_inc(S("level_q"), 1)

            level = C("level").rearrange("p (j n) -> p j n", n=P)

            def level_scores(j):
                if j == 7:
                    for g in range(2):
                        b = take(("lv", j, g))
                        free(v.tensor_copy(PH[:, 4 * g:4 * g + 4, P:TP], b[:, :].rearrange("p (h n) -> p h n", n=P)))
                    return
                for h in range(0, HG, 2):
                    b = take(("lv", j, h))
                    for q in range(2):
                        for i in range(2):
                            at = 0 if i == 0 else TP
                            ins = v.copy_predicated(PH[:, h + q, at:at + P], level[:, j, :].bitcast(mybir.dt.uint32),
                                                    b[:, (2 * q + i) * P:(2 * q + i + 1) * P])
                    free(ins)
                if j < 3:
                    b = take(("lv", j, "s"))
                    mask = level[0:SMP, j, 0:SMP].bitcast(mybir.dt.uint32)
                    for h in range(HG):
                        ins = v.copy_predicated(PH[0:SMP, h, 384:448], mask, b[0:SMP, h * SMP:(h + 1) * SMP])
                    free(ins)

            def same_scores():
                for h in range(0, HG, 2):
                    b = take(("diag", h))
                    bv = b[:, :].rearrange("p (h i n) -> p h i n", i=2, n=P)
                    for q in range(2):
                        v.tensor_tensor(PH[:, h + q, 0:P], bv[:, q, 0, :], ident, ALU.mult)
                        ins = v.tensor_tensor(PH[:, h + q, TP:384], bv[:, q, 1, :], ident, ALU.mult)
                    free(ins)
                b = take(("diag", "s"))
                free(v.tensor_tensor(PH[0:SMP, :, 384:448], b[0:SMP, :].rearrange("p (h n) -> p h n", n=SMP),
                                     ident[0:SMP, 0:SMP].unsqueeze(1).to_broadcast([SMP, HG, SMP]), ALU.mult))

            for c in C_ORDER:
                for half in range(2):
                    if c in (2, 3):
                        for j in range(2):
                            forget(4 * (c - 2) + 2 * half + j)
                    if c in (4, 5):
                        values(1, c - 4, half)
                    split_dense()
                    if c >= 4:
                        i = 2 * (c - 4) + half
                        if i == 0:
                            after_empty(dve, ("c", 1, 3))
                        level_queries(7 - i)
                        if i == 0:
                            same_scores()
                        else:
                            level_scores(8 - i)
                        if i < 7:
                            level_differences(6 - i)
                if c == 1:
                    for h in range(HG):
                        dve.wait_ge(S("forget_ln"), h + 1)
                        ins = v.tensor_tensor_scan(CUM[:, h, :], C("reset"), LV[1][:, h, :], 0.0, ALU.mult, ALU.add)
                    step(ins)
                    level_differences(7)
            end = LV[1]
            v.tensor_tensor(end[:, :, 0:TP], CUM[:, :, TP - 1:TP].to_broadcast([P, HG, TP]), CUM[:, :, 0:TP], ALU.subtract)
            for h in range(HG):
                cs = CUM[:, h, TP:NT].rearrange("p (b t) -> p b t", t=TS)
                ins = v.tensor_tensor(end[:, h, TP:NT].rearrange("p (b t) -> p b t", t=TS),
                                      cs[:, :, TS - 1:TS].to_broadcast([P, NB, TS]), cs, ALU.subtract)
            ins.then_inc(S("end_diff"), 1)
            level_scores(0)
            dve.wait_ge(S("end_exp"), 2)
            for h in range(HG):
                v.tensor_tensor(K[:, h, :], K[:, h, :], end[:, h, :], ALU.mult).then_inc(S("hgrn_kend"), 1)
                v.tensor_tensor(Q[:, h, TP:NT], Q[:, h, TP:NT], ES[:, h, :], ALU.mult).then_inc(S("qe1"), 1)
            for u in range(HG + 1):
                if u > 0:
                    w = u - 1
                    free(v.tensor_copy(OH[:, w, :], take(("num", 1, w))[:, 0:NT]))
                    dec = ES[:, w, :].rearrange("p (b t) -> p b t", t=TS)[:, :, TS - 1]
                    new_states(1, w, lambda q: dec[:, q:q + 1])
                    dve.wait_ge(S("hn1_squares"), w + 1)
                    v.scalar_tensor_tensor(out=OH[:, w, :], in0=OH[:, w, :], scalar=prow("hg_gn", w), in1=G[:, w, :],
                                           op0=ALU.mult, op1=ALU.mult).then_inc(S("gated1"), 1)
            dve.wait_ge(S("gated1"), HG)
            mix(OH, "hn1", lambda u: None, HL_O)
            projected_out("oc")
            normed("n3", "ln_ffn", 8, hT)

            step(v.memset(LG[:, :, :], 0.0))
            b = take("logits")
            v.tensor_copy(LG[:, 0:2, :], b[:, 0:16].rearrange("p (i e) -> p i e", e=NE))
            free(v.tensor_copy(LG[0:SMP, 2, :], b[0:SMP, 16:24]))
            after_empty(dve, "logits")
            c1 = CMP[:, :, :].rearrange("p i (e f) -> p (i e) f", f=NE)
            c2 = CM2[:, :, :].rearrange("p i (e f) -> p (i e) f", f=NE)
            for i in range(3):
                other = LG[:, i, :].unsqueeze(1).to_broadcast([P, NE, NE])
                me = LG[:, i, :].unsqueeze(2).to_broadcast([P, NE, NE])
                v.tensor_tensor(c1[:, i * NE:(i + 1) * NE, :], other, me, ALU.is_gt)
                v.tensor_tensor(c2[:, i * NE:(i + 1) * NE, :], other, me, ALU.is_equal)
            v.reduce_max(V1[:, :], LG[:, :, :], AX.X)
            step(v.memset(RND[:, :], 0.0))
            step(v.tensor_tensor(CM2[:, :, :], CM2[:, :, :], C("tie").unsqueeze(1).to_broadcast([P, 3, 64]), ALU.mult))
            step(v.tensor_tensor(CMP[:, :, :], CMP[:, :, :], CM2[:, :, :], ALU.add))
            step(v.tensor_reduce(SELM[:, :, :].rearrange("p i e -> p (i e)"), c1, AX.X, ALU.add))
            v.tensor_scalar(SELM[:, :, :], SELM[:, :, :], 1.5, None, ALU.is_lt).then_inc(S("chosen"), 1)
            v.tensor_tensor(GATE[:, :, :], LG[:, :, :], V1[:, :].unsqueeze(2).to_broadcast([P, 3, NE]),
                            ALU.subtract).then_inc(S("router_diff"), 1)
            dve.wait_ge(S("router_exp"), 1)
            dve.wait_ge(S("chosen"), 1)
            step(v.tensor_tensor(GATE[:, :, :], GATE[:, :, :], SELM[:, :, :], ALU.mult))
            step(v.tensor_reduce(V1[:, :], GATE[:, :, :], AX.X, ALU.add))
            step(v.reciprocal(V1[:, :], V1[:, :]))
            step(v.tensor_tensor(GATE[:, :, :], GATE[:, :, :], V1[:, :].unsqueeze(2).to_broadcast([P, 3, NE]), ALU.mult))
            b = take("ranks")
            step(v.memset(RANK[:, :, :], -BIG))
            for i, (t0, tn) in enumerate(BLK):
                step(v.scalar_tensor_tensor(out=RANK[0:tn, i, :], in0=b[0:tn, i * NE:(i + 1) * NE], scalar=BIG,
                                            in1=SELM[0:tn, i, :], op0=ALU.add, op1=ALU.mult))
                step(v.tensor_scalar(RANK[0:tn, i, :], RANK[0:tn, i, :], -BIG, None, ALU.add))
            free(v.reduce_max(RND[:, 0:1], b[:, 24:32], AX.X))
            after_empty(dve, "ranks")
            v.tensor_scalar(RND[:, 1:2], RND[:, 0:1], CAP + 0.5, 8.0, ALU.is_gt, ALU.mult)
            step(v.tensor_scalar(RND[:, 2:3], RND[:, 0:1], 2 * CAP + 0.5, 8.0, ALU.is_gt, ALU.mult))
            step(v.tensor_tensor(RND[:, 3:4], RND[:, 1:2], RND[:, 2:3], ALU.add))
            v.tensor_scalar(NIT[0:1, 0:1], RND[0:1, 3:4], float(NE), None, ALU.add).then_inc(S("rounds_known"), 1)

            def select(dst, e, gated):
                for i, (t0, tn) in enumerate(BLK):
                    rank = RANK[0:tn, i, bass.ds(e, 1)]
                    if gated:
                        ins = v.tensor_scalar(dst[0:tn, i, :], C("slots", tn), rank, GATE[0:tn, i, bass.ds(e, 1)],
                                              ALU.is_equal, ALU.mult)
                    else:
                        ins = v.tensor_scalar(dst[0:tn, i, :], C("slots", tn), rank, None, ALU.is_equal)
                return ins

            def gathered():
                for g in range(2):
                    hi, lo = [X[:, 4 * g:4 * g + 4, :].rearrange("p k n -> p (k n)") for X in (XGH, XGL)]
                    v.tensor_copy(hi, banks[6 + g][:, :]).then_inc(S("xg_hi"), 1)
                for g in range(2):
                    hi, lo = [X[:, 4 * g:4 * g + 4, :].rearrange("p k n -> p (k n)") for X in (XGH, XGL)]
                    if g == 0:
                        dve.wait_ge(S("xg_hi"), xg_done + 2)
                    v.tensor_tensor(lo, banks[6 + g][:, :], hi.bitcast(F32), ALU.subtract).then_inc(S("misc_done"), 1)

            select(SE, 0, False).then_inc(S("sel_ready"), 1)
            after_empty(dve, ("hn", 2, 1))
            v.memset(banks[2][:, :], 0.0)
            v.memset(banks[3][:, :], 0.0).then_inc(S("down_zero"), 1)
            v.memset(STH[:, :].bitcast(F32), 0.0)
            v.memset(GS[:, :], 0.0).then_inc(S("gates_ready"), 1)
            xg_done = 0
            dve.wait_ge(S("misc_full"), 2)
            gathered()

            def split_low(done, p):
                dve.wait_ge(S("unit_hi"), done * NU + p + 1)
                v.tensor_tensor(WL[p % NSPLIT][:, :], STAGE[:, p % NSTAGE, :], WH[p % NSPLIT][:, :].bitcast(F32),
                                ALU.subtract).then_inc(S("unit_split"), 1)

            def y_low(done):
                dve.wait_ge(S("gates_ready"), done + 1)
                dve.wait_ge(S("y_hi"), done + 1)
                for g in range(2):
                    at = slice(g * 512, (g + 1) * 512)
                    ins = v.scalar_tensor_tensor(out=YL[:, at], in0=banks[2 + g][:, :], scalar=GS[:, 0:1],
                                                 in1=YH[:, at].bitcast(F32), op0=ALU.mult, op1=ALU.subtract)
                ins.then_inc(S("y_ready"), 1)

            def scattered(done, ms=range(KD)):
                for m in ms:
                    dve.wait_ge(S("misc_full"), done * 10 + m + 3)
                    v.tensor_tensor(xT[:, m, :], xT[:, m, :], banks[6 + m % 2][:, 0:NT],
                                    ALU.add).then_inc(S("misc_done"), 1)

            dve.wait_ge(S("rounds_known"), 1)
            rounds = dve.value_load(NIT[0:1, 0:1], min_val=NE, max_val=3 * NE)
            with dve.Fori(0, rounds) as it:
                e = it & (NE - 1)
                e1 = (it + 1) & (NE - 1)

                def product(c):
                    dve.wait_ge(S("silu_done"), it * NFC + c + 1)
                    if c >= 2:
                        dve.wait_ge(S("t_full"), it * 12 + c - 1)
                    v.tensor_tensor(AN[:, c % 2, :], SL[:, c % 2, :], banks[c % 2][:, FC:2 * FC],
                                    ALU.mult).then_inc(S("a_ready"), 1)

                def turned(c):
                    dve.wait_ge(S("at_hi"), it * NFC + c + 1)
                    v.tensor_tensor(ATL[:, c % 2, :], banks[4 + c % 2][:, 0:FC], ATH[:, c % 2, :].bitcast(F32),
                                    ALU.subtract).then_inc(S("t_copied"), 1)

                for p in range(NSPLIT):
                    split_low(it, p)
                y_low(it)
                dve.wait_ge(S("misc_done"), it * 10 + 2)
                select(SGE, e, True).then_inc(S("sge_ready"), 1)
                select(SE, e1, False).then_inc(S("sel_ready"), 1)
                for p, (kind, c) in enumerate(UNITS):
                    if kind == "d" and c < NFC - 2:
                        turned(c + 1)
                    if p + NSPLIT < NU:
                        split_low(it, p + NSPLIT)
                    if kind == "b":
                        product(c)
                    if kind == "b" and 1 <= c <= 4:
                        scattered(it, (2 * c - 2, 2 * c - 1))
                    if kind == "b" and c == 1:
                        turned(0)
                    if kind == "d" and c == 0:
                        dve.wait_ge(S("sge_ready"), it + 1)
                        for i in range(3):
                            r = RANK[:, i, bass.ds(e, 1)]
                            v.tensor_scalar(r, r, -float(CAP), None, ALU.add)
                    if kind == "d" and c == NFC - 3:
                        xg_done = it * 2 + 2
                        dve.wait_ge(S("misc_full"), it * 10 + 12)
                        gathered()
                        turned(NFC - 1)
                        dve.wait_ge(S("t_full"), it * 12 + NFC + 1)
                        turned_selection = banks[4 + NFC % 2][:, 0:NT]
                        v.reduce_max(GS[:, :], turned_selection, AX.X).then_inc(S("gates_ready"), 1)
                        v.tensor_scalar(STH[:, :], turned_selection, 0.0, None, ALU.is_gt).then_inc(S("t_copied"), 1)
            y_low(rounds)
            scattered(rounds)
            dve.wait_ge(S("misc_done"), rounds * 10 + 10)
            normed("n4", "ln_final", 0, hT)

        @block.gpsimd
        def _(pool):
            g = nc.gpsimd
            g.memset(XC[:, :, 0:3], 0.0).then_inc(S("history_zero"), 1)

            def src_of(layer, u):
                if layer:
                    return A["state_hgrn"][0, :, u]
                return A["state_ret"][0, :, u] if u < H4 else A["state_mlstm_c"][0, :, u - H4]

            def dst_of(layer, u):
                if layer:
                    return O["hg_s"][0, :, u]
                return O["ret_s"][0, :, u] if u < H4 else O["mc_s"][0, :, u - H4]

            def load_state(layer, u):
                pool.dma_start(ST[:, u % NST], src_of(layer, u).rearrange("b k v -> k b v")).then_inc(
                    S(f"state_in_{layer}_{u % NST}"), 16)

            def store_state(layer, u):
                after_empty(pool, ("ss", layer, u, 1))
                pool.dma_start(dst_of(layer, u).rearrange("b k v -> k b v"), ST[:, u % NST]).then_inc(
                    S(f"state_out_{u % NST}"), 16)

            def spread(layer, u):
                if u >= 1:
                    after_fill(pool, ("ss", layer, u - 1, 1))
                v1 = V[0:SMP, 2, u * DH:(u + 1) * DH].unsqueeze(1).to_broadcast([SMP, NB, DH])
                m = C("bmask", SMP).unsqueeze(2).to_broadcast([SMP, NB, DH])
                g.tensor_tensor(VX[0:SMP], v1, m, ALU.mult).then_inc(S(f"vx{layer}"), 1)

            for u in range(NST):
                load_state(0, u)
            pool.wait_ge(S("conv_sum"), 1)
            pool.wait_ge(S("history_zero"), 1)
            g.tensor_copy(CT[:, :, 0:3], XC[:, :, TP:SX])
            for k in range(KD):
                tail = XC[:, k, SX:XW].rearrange("p (b t) -> p b t", t=3 + TS)[:, :, TS:TS + 3]
                ins = g.tensor_copy(CT[:, k, 3:27].rearrange("p (b t) -> p b t", t=3), tail)
            ins.then_inc(S("conv_tail"), 1)
            pool.wait_ge(S("conv_silu"), KD)
            g.tensor_scalar(K[:, H4:KD, :], K[:, H4:KD, :], DH ** -0.5, None, ALU.mult).then_inc(S("keys_scaled"), 1)
            after_empty(pool, (("V", 0, 0), 1, 2))
            stored = [0] * NST
            for layer in range(2):
                if layer:
                    for j in range(7, -1, -1):
                        pool.wait_ge(S("level_exp"), 8 - j)
                        ls, ks = halves(LV[j % 2], j)[0], halves(K, j)[0]
                        g.tensor_tensor(ls, ls, ks, ALU.mult).then_inc(S("level_k"), 1)
                    after_empty(pool, (("V", 1, 1), 1, 2))
                    after_fill(pool, ("c", 7, 3))
                    for u in range(NST):
                        pool.wait_ge(S(f"state_out_{u}"), 16 * stored[u])
                        load_state(1, u)
                for u in range(KD + 1):
                    if u < KD:
                        spread(layer, u)
                    if u > 0:
                        store_state(layer, u - 1)
                        stored[(u - 1) % NST] += 1
                        if u - 1 + NST < KD:
                            pool.wait_ge(S(f"state_out_{(u - 1) % NST}"), 16 * stored[(u - 1) % NST])
                            load_state(layer, u - 1 + NST)
            for i, (t0, tn) in enumerate(BLK):
                pool.wait_ge(S("hn_hi"), i + 1)
                g.tensor_tensor(HNL[0:tn, i, :], HN[0:tn, i, :], HNH[0:tn, i, :].bitcast(F32),
                                ALU.subtract).then_inc(S("hn_split"), 1)
            for s in range(NST):
                pool.wait_ge(S(f"state_out_{s}"), 16 * stored[s])


_IN = ["x_prompt", "x_sample", "state_ret", "state_mlstm_c", "state_mlstm_n", "state_mlstm_m", "state_conv",
       "state_hgrn", "ln_mix", "ln_ffn", "ln_final", "w_in_ab", "b_gates_ab", "conv_w_ab", "conv_b_ab", "ret_gn",
       "ml_gn", "w_out_ab", "w_in_c", "hg_lower", "hg_gn", "w_out_c", "w_ffn_gate", "w_ffn_up", "w_ffn_down",
       "w_router", "b_router", "w_moe_gate", "w_moe_up", "w_moe_down"]
_OUT = [("y_prompt", (1, TP, D)), ("y_sample", (NB, TS, D)),
        ("ret_p", (1, 1, 4, DH, DH)), ("ret_s", (1, NB, 4, DH, DH)),
        ("mc_p", (1, 1, 4, DH, DH)), ("mc_s", (1, NB, 4, DH, DH)),
        ("mn_p", (1, 1, 4, DH)), ("mn_s", (1, NB, 4, DH)),
        ("mm_p", (1, 1, 4)), ("mm_s", (1, NB, 4)),
        ("conv_p", (1, 1, 3, D)), ("conv_s", (1, NB, 3, D)),
        ("hg_p", (1, 1, HG, DH, DH)), ("hg_s", (1, NB, HG, DH, DH))]


def kernel(**inputs):
    import concourse.bacc as bacc
    from concourse.bass_utils import run_bass_kernel_spmd

    nc = bacc.Bacc("TRN2", target_bir_lowering=False, num_devices=1)
    arrays = {f"in_{name}": np.ascontiguousarray(inputs[name]) for name in _IN}
    arrays["in_cst"] = constants()
    ins = {name[3:]: nc.dram_tensor(name, a.shape, F32, kind="ExternalInput").ap() for name, a in arrays.items()}
    outs = {name: nc.dram_tensor(f"out_{name}", shape, F32, kind="ExternalOutput").ap() for name, shape in _OUT}
    trunk_kernel(nc, ins, outs)
    r = run_bass_kernel_spmd(nc, [arrays], core_ids=[0])
    return tuple(r.results[0][f"out_{name}"] for name, _ in _OUT)
```
